# Optimizing a Trainium2 kernel written in Bass

```python
import jax, jax.numpy as jnp
from jax import lax
import numpy as np

D_MODEL = 2048
BATCH = 1
SEQ = 256
DEPTH = 1

CHUNK = 64
Q_BLOCK = 128
MEM_LEN = 256
EPS = 1e-6

CONV_WIDTH = 1024
SHORT_CONV_K = 3
DIFF_HEADS = 8
DIFF_QK_DIM = 64
DIFF_V_DIM = 2 * DIFF_QK_DIM
DIFF_QK_WIDTH = DIFF_HEADS * 2 * DIFF_QK_DIM
DIFF_WIDTH = DIFF_HEADS * DIFF_V_DIM
CROSS_HEADS = 4
CROSS_HEAD_DIM = 256
CROSS_WIDTH = CROSS_HEADS * CROSS_HEAD_DIM
N_BRANCH = 3
D_FF = 5632
FFN_CONV_K = 3

IN_SPLITS = (CONV_WIDTH, CONV_WIDTH, CONV_WIDTH, DIFF_QK_WIDTH, DIFF_QK_WIDTH, DIFF_WIDTH, CROSS_WIDTH)
IN_WIDTH = sum(IN_SPLITS)
IN_OFFSETS = tuple(int(o) for o in np.cumsum(IN_SPLITS)[:-1])

kernel_name = "hybrid_gated_conv_diffattn_memxattn_block"

def rmsnorm(x, g):
    xf = x.astype(jnp.float32)
    y = xf * lax.rsqrt(jnp.mean(xf * xf, axis=-1, keepdims=True) + EPS)
    return (y * g.astype(jnp.float32)).astype(x.dtype)

def causal_dwconv(u, w):
    k = w.shape[0]
    return lax.conv_general_dilated(
        u, w[:, None, :].astype(u.dtype), window_strides=(1,), padding=[(k - 1, 0)],
        dimension_numbers=("NWC", "WIO", "NWC"), feature_group_count=u.shape[-1])

def short_conv_mixer(b, c, v, conv_w):
    return b * causal_dwconv(c * v, conv_w)

def diff_attention(q, k, v, lq1, lk1, lq2, lk2, g_sub, lambda_init):
    bsz, seq = q.shape[0], q.shape[1]
    n_blocks = seq // Q_BLOCK
    lam = (jnp.exp(jnp.sum(lq1.astype(jnp.float32) * lk1.astype(jnp.float32)))
           - jnp.exp(jnp.sum(lq2.astype(jnp.float32) * lk2.astype(jnp.float32)))
           + lambda_init)
    qh = q.transpose(0, 2, 3, 1, 4)
    kh = k.transpose(0, 2, 3, 1, 4)
    vh = v.transpose(0, 2, 1, 3)
    q_blocks = jnp.moveaxis(
        qh.reshape(bsz, DIFF_HEADS, 2, n_blocks, Q_BLOCK, DIFF_QK_DIM), 3, 0)
    key_chunk = jnp.arange(seq, dtype=jnp.int32) // CHUNK
    scale = DIFF_QK_DIM ** -0.5

    def block(args):
        qb, start = args
        s = jnp.einsum("bhcqd,bhckd->bhcqk", qb, kh,
                       preferred_element_type=jnp.float32) * scale
        q_chunk = (start + jnp.arange(Q_BLOCK, dtype=jnp.int32)) // CHUNK
        mask = key_chunk[None, :] <= q_chunk[:, None]
        p = jax.nn.softmax(jnp.where(mask, s, -jnp.inf), axis=-1)
        a = p[:, :, 0] - lam * p[:, :, 1]
        return jnp.einsum("bhqk,bhkd->bhqd", a.astype(vh.dtype), vh)

    starts = jnp.arange(n_blocks, dtype=jnp.int32) * Q_BLOCK
    o = lax.map(block, (q_blocks, starts))
    o = o.transpose(1, 0, 3, 2, 4).reshape(bsz, seq, DIFF_HEADS, DIFF_V_DIM)
    o = rmsnorm(o, g_sub) * (1.0 - lambda_init)
    return o.reshape(bsz, seq, DIFF_WIDTH)

def memory_cross_attention(q, mem_n, w_kv):
    bsz, seq = q.shape[0], q.shape[1]
    kv = mem_n @ w_kv
    k, v = jnp.split(kv, 2, axis=-1)
    k = k.reshape(bsz, -1, CROSS_HEADS, CROSS_HEAD_DIM)
    v = v.reshape(bsz, -1, CROSS_HEADS, CROSS_HEAD_DIM)
    s = jnp.einsum("bqhd,bkhd->bhqk", q, k, preferred_element_type=jnp.float32) * CROSS_HEAD_DIM ** -0.5
    p = jax.nn.softmax(s, axis=-1)
    o = jnp.einsum("bhqk,bkhd->bqhd", p.astype(v.dtype), v)
    return o.reshape(bsz, seq, CROSS_WIDTH)

def setup_inputs(seed: int = 0) -> dict:
    key = jax.random.key(seed)
    ks = jax.random.split(key, 26)

    def nrm(k, shape, scale):
        return jax.random.normal(k, shape, jnp.float32) * scale

    def gain(k, shape):
        return 1.0 + 0.05 * jax.random.normal(k, shape, jnp.float32)

    L, D = DEPTH, D_MODEL
    return {
        "x": nrm(ks[0], (BATCH, SEQ, D), 1.0),
        "mem": nrm(ks[1], (BATCH, MEM_LEN, D), 1.0),
        "g_mix_pre": gain(ks[2], (L, D)),
        "w_in": nrm(ks[3], (L, D, IN_WIDTH), D ** -0.5),
        "w_gate": nrm(ks[4], (L, D, N_BRANCH * D), D ** -0.5),
        "b_gate": nrm(ks[5], (L, N_BRANCH * D), 0.02),
        "conv_w": nrm(ks[6], (L, SHORT_CONV_K, CONV_WIDTH), SHORT_CONV_K ** -0.5),
        "w_conv_out": nrm(ks[7], (L, CONV_WIDTH, D), CONV_WIDTH ** -0.5),
        "lambda_q1": nrm(ks[8], (L, DIFF_QK_DIM), 0.1),
        "lambda_k1": nrm(ks[9], (L, DIFF_QK_DIM), 0.1),
        "lambda_q2": nrm(ks[10], (L, DIFF_QK_DIM), 0.1),
        "lambda_k2": nrm(ks[11], (L, DIFF_QK_DIM), 0.1),
        "g_diff_sub": gain(ks[12], (L, DIFF_V_DIM)),
        "w_diff_out": nrm(ks[13], (L, DIFF_WIDTH, D), DIFF_WIDTH ** -0.5),
        "g_mem": gain(ks[14], (L, D)),
        "w_mem_kv": nrm(ks[15], (L, D, 2 * CROSS_WIDTH), D ** -0.5),
        "w_cross_out": nrm(ks[16], (L, CROSS_WIDTH, D), CROSS_WIDTH ** -0.5),
        "w_o": nrm(ks[17], (L, D, D), D ** -0.5),
        "g_mix_post": gain(ks[18], (L, D)),
        "g_ffn_pre": gain(ks[19], (L, D)),
        "w_up": nrm(ks[20], (L, D, 2 * D_FF), D ** -0.5),
        "ffn_conv_w": nrm(ks[21], (L, FFN_CONV_K, 2 * D_FF), FFN_CONV_K ** -0.5),
        "w_down": nrm(ks[22], (L, D_FF, D), D_FF ** -0.5),
        "g_ffn_post": gain(ks[23], (L, D)),
    }

def reference(x, mem, g_mix_pre, w_in, w_gate, b_gate, conv_w, w_conv_out,
              lambda_q1, lambda_k1, lambda_q2, lambda_k2, g_diff_sub, w_diff_out,
              g_mem, w_mem_kv, w_cross_out, w_o, g_mix_post,
              g_ffn_pre, w_up, ffn_conv_w, w_down, g_ffn_post):
    bsz, seq = x.shape[0], x.shape[1]
    for l in range(DEPTH):
        lambda_init = 0.8 - 0.6 * float(np.exp(-0.3 * l))
        h = rmsnorm(x, g_mix_pre[l])
        proj = h @ w_in[l]
        cb, cc, cv, dq, dk, dv, xq = jnp.split(proj, IN_OFFSETS, axis=-1)

        y_conv = short_conv_mixer(cb, cc, cv, conv_w[l]) @ w_conv_out[l]

        y_diff = diff_attention(
            dq.reshape(bsz, seq, DIFF_HEADS, 2, DIFF_QK_DIM),
            dk.reshape(bsz, seq, DIFF_HEADS, 2, DIFF_QK_DIM),
            dv.reshape(bsz, seq, DIFF_HEADS, DIFF_V_DIM),
            lambda_q1[l], lambda_k1[l], lambda_q2[l], lambda_k2[l],
            g_diff_sub[l], lambda_init) @ w_diff_out[l]

        y_cross = memory_cross_attention(
            xq.reshape(bsz, seq, CROSS_HEADS, CROSS_HEAD_DIM),
            rmsnorm(mem, g_mem[l]), w_mem_kv[l]) @ w_cross_out[l]

        gates = jax.nn.sigmoid(h @ w_gate[l] + b_gate[l])
        g_a, g_b, g_c = jnp.split(gates, N_BRANCH, axis=-1)
        merged = g_a * y_conv + g_b * y_diff + g_c * y_cross
        x = x + rmsnorm(merged @ w_o[l], g_mix_post[l])

        h = rmsnorm(x, g_ffn_pre[l])
        u = causal_dwconv(h @ w_up[l], ffn_conv_w[l])
        gate, val = jnp.split(u, 2, axis=-1)
        x = x + rmsnorm((jax.nn.silu(gate) * val) @ w_down[l], g_ffn_post[l])
    return x


_drawn_inputs = setup_inputs


def setup_inputs(seed=0):
    import zlib

    import numpy as np

    out = dict(_drawn_inputs(seed))
    spreads = {}
    factors = {'b_gate': 8.0, 'lambda_k1': 8.0, 'lambda_q2': 8.0, 'g_mem': 8.0}
    for name, (base, spread) in spreads.items():
        noise = np.random.default_rng([zlib.crc32(name.encode()), seed]).standard_normal(out[name].shape)
        drawn = base * np.exp(spread * noise) if base else spread * noise
        out[name] = __import__('jax').numpy.asarray(drawn.astype(out[name].dtype))
    for name, factor in factors.items():
        out[name] = (out[name] * factor).astype(out[name].dtype)
    return out
```

```python
from contextlib import ExitStack

import concourse.bass as bass
from concourse import mybir

F32 = mybir.dt.float32
F32R = mybir.dt.float32r
ALU = mybir.AluOpType
ACT = mybir.ActivationFunctionType
AX = mybir.AxisListType

P = 128
NT = 2
TOK = NT * P
CW = 512
BPC = CW // P
KB = 2
RING = 4
EPS = 1e-6
LAMBDA_INIT = 0.8 - 0.6 * 1.0
SWISH_EXP = -0.5


def build_block_kernel(nc, x, mem, g_mix_pre, w_in, w_gate, b_gate, conv_w, w_conv_out,
                       lambda_q1, lambda_k1, lambda_q2, lambda_k2, g_diff_sub, w_diff_out,
                       g_mem, w_mem_kv, w_cross_out, w_o, g_mix_post,
                       g_ffn_pre, w_up, ffn_conv_w, w_down, g_ffn_post, out):
    D = x.shape[2]
    CONV = conv_w.shape[2]
    FF = w_down.shape[1]
    CROSS = w_cross_out.shape[1]
    DIFF = w_diff_out.shape[1]
    DH, DQK = 8, 64
    CH, CHD = 4, CROSS // 4
    DK = D // P
    HK = CONV // P
    FK = FF // P
    NCH = D // CW
    NUP = FF // CW
    GATE_OF = (0, 2, 1)
    assert x.shape[1] == TOK and mem.shape[1] == TOK and DIFF == DH * P and CONV == DIFF == CROSS

    in_cols = {"cb": 0, "cc": CONV, "cv": 2 * CONV, "dq": 3 * CONV, "dk": 4 * CONV, "dv": 5 * CONV, "xq": 6 * CONV}
    proj = [("mv", 0), ("mv", 1), ("mk", 0), ("mk", 1), ("xq", 0), ("xq", 1),
            ("cc", 0), ("cv", 0), ("cc", 1), ("cv", 1), ("cb", 0), ("cb", 1),
            ("dq", 0), ("dq", 1), ("dk", 0), ("dk", 1), ("dv", 0), ("dv", 1)]
    NP = len(proj)
    turned = [p for p in proj if p[0] in ("mk", "xq", "cv", "cb", "dq", "dk")]
    TI = {p: k for k, p in enumerate(turned)}
    CROSS_STEP = 7
    T_MERGE = len(turned)
    T_UP = T_MERGE + NCH

    CB = DK // KB
    OB = HK // KB
    DB = FK // KB
    DBV = -(-DB // RING) * RING
    SB = CB + OB
    N_BR = NP * CB
    N_O = N_BR + 3 * NCH * SB
    N_UP = N_O + NCH * CB
    N_DN = N_UP + 2 * NUP * CB
    E_BR = NP // 2
    E_O = E_BR + 3 * NCH
    E_UP = E_O + NCH // 2
    E_DN = E_UP + NUP

    with ExitStack() as ctx:
        def sem(name):
            return ctx.enter_context(nc.semaphore(name))

        K = 1024
        base = -(-nc.sbuf_base // 32) * 32
        CONST, CONST_SIZE = 48 * K, 3 * K + 512
        RA = CONST + CONST_SIZE
        RB = RA + 32 * K
        RD = RB + 32 * K
        RC = RD + 76 * K
        ctx.enter_context(nc.sbuf_tensor("arena", [P, (RC + 16 * K) // 4], F32))

        def at(name, offset, shape, dt=F32):
            return nc.alloc_sbuf_tensor_at(name, shape, dt, offset=base + offset)

        raw = [at(f"raw{s}", 4 * K * s, [P, KB, CW]) for s in range(RING)]
        w_hi = [at(f"w_hi{s}", 16 * K + 4 * K * s, [P, KB, CW], F32R) for s in range(RING)]
        w_lo = [at(f"w_lo{s}", 32 * K + 4 * K * s, [P, KB, CW], F32R) for s in range(RING)]

        cpos = [CONST]

        def const(name, shape):
            n = 4
            for d in shape[1:]:
                n *= d
            o = cpos[0]
            cpos[0] += -(-n // 32) * 32
            assert cpos[0] <= CONST + CONST_SIZE
            return at(name, o, shape)

        ident = const("ident", [P, P])
        vecs = const("vecs", [P, 3 * DK + 3 * HK + 1])
        up_taps = const("up_taps", [P, 3, 2 * FK])
        g_sub = const("g_sub", [P, 1])
        minus_half = const("minus_half", [P, NT])
        lam_dots = const("lam_dots", [P, 2])
        lam_exp = const("lam_exp", [P, 2])
        minus_lam = const("minus_lam", [P, 1])
        sq_mem = const("sq_mem", [P, NT])
        sq_x = const("sq_x", [P, NT])
        mean_sq = const("mean_sq", [P, NT])
        r_mem = const("r_mem", [P, NT])
        r_x = const("r_x", [P, NT])
        r_mix = const("r_mix", [P, NT])
        r_h2 = const("r_h2", [P, NT])
        r_out = const("r_out", [P, NT])
        sq_part = const("sq_part", [P, NT, NCH])
        sq_mix = const("sq_mix", [P, NT])
        sq_h2 = const("sq_h2", [P, NT])
        sq_part2 = const("sq_part2", [P, NT, NCH])
        sq_down = const("sq_down", [P, NT])
        top = const("top", [P, NT, 2])
        neg_top = const("neg_top", [P, NT, 2])
        psum_e = const("psum_e", [P, NT, 2])
        inv_e = const("inv_e", [P, NT, 2])
        lam_inv = const("lam_inv", [P, NT])
        sq_o = const("sq_o", [P, NT])
        ms_o = const("ms_o", [P, NT])
        r_o = const("r_o", [P, NT])
        g_pre_v, g_mem_v, g_ffn_v = vecs[:, 0:DK], vecs[:, DK:2 * DK], vecs[:, 2 * DK:3 * DK]
        taps_v = vecs[:, 3 * DK:3 * DK + 3 * HK]

        hT_hi = at("hT_hi", RA, [P, DK, TOK], F32R)
        hT_lo = at("hT_lo", RA + 16 * K, [P, DK, TOK], F32R)
        h2_hi, h2_lo = hT_hi, hT_lo
        y_down = at("y_down", RA, [P, NT, D])
        g_last = at("g_last", RA + 16 * K, [P, D])
        memT_hi = at("memT_hi", RB, [P, DK, TOK], F32R)
        memT_lo = at("memT_lo", RB + 16 * K, [P, DK, TOK], F32R)
        qT = at("qT", RB, [P, HK, TOK])
        kT = at("kT", RB + 8 * K, [P, HK, TOK])
        v_tok = at("v_tok", RB + 16 * K, [P, NT, DIFF])
        xqT = at("xqT", RB + 24 * K, [P, HK, TOK])
        mixT_hi = at("mixT_hi", RB, [P, DK, TOK], F32R)
        mixT_lo = at("mixT_lo", RB + 16 * K, [P, DK, TOK], F32R)
        mem_sb = at("mem_sb", RC, [P, NT, D])
        y_conv_hi = at("y_conv_hi", RC, [P, HK, TOK], F32R)
        y_conv_lo = at("y_conv_lo", RC + 8 * K, [P, HK, TOK], F32R)
        x_res = at("x_res", RC, [P, NT, D])
        x_sb = at("x_sb", RD, [P, NT, D])
        y_diff_hi = at("y_diff_hi", RD, [P, HK, TOK], F32R)
        y_diff_lo = at("y_diff_lo", RD + 8 * K, [P, HK, TOK], F32R)
        y_mix = at("y_mix", RD, [P, NT, D])
        mkT = at("mkT", RD + 16 * K, [P, HK, TOK])
        mv_tok = at("mv_tok", RD + 24 * K, [P, NT, CROSS])
        merged = at("merged", RD + 16 * K, [P, NT, D])
        stage = at("stage", RD + 32 * K, [P, NT, CW])
        y_cross_hi = at("y_cross_hi", RD + 36 * K, [P, HK, TOK], F32R)
        y_cross_lo = at("y_cross_lo", RD + 44 * K, [P, HK, TOK], F32R)
        g_post = at("g_post", RD + 36 * K, [P, D])
        cc_sb = at("cc_sb", RD + 52 * K, [P, NT, CW])
        convT = at("convT", RD + 56 * K, [P, HK, TOK])
        y_tmp = at("y_tmp", RD + 64 * K, [P, BPC, TOK])
        p_cross = at("p_cross", RD + 68 * K, [P, NT, TOK])
        p_crossT = at("p_crossT", RD + 70 * K, [P, NT, TOK])
        vec_rows = at("vec_rows", RD + 52 * K, [P, P])
        up_rows = at("up_rows", RD + 53 * K, [P, 3, P])
        lam_rows = at("lam_rows", RD + 55 * K, [P, 4, DQK])
        lam_prod = at("lam_prod", RD + 56 * K, [P, 2, DQK])
        gate_pre = at("gate_pre", RD + 52 * K, [P, NT, CW])
        gate_tanh = at("gate_tanh", RD + 56 * K, [P, NT, CW])
        gated = at("gated", RD + 60 * K, [P, NT, CW])
        bias_bc = at("bias_bc", RD + 64 * K, [P, CW])
        qk_head = at("qk_head", RD + 66 * K, [P, 2, TOK])
        p_diff = at("p_diff", RD + 68 * K, [P, 2, 3 * P])
        a_diff = at("a_diff", RD + 71 * K, [P, 3 * P])
        a_diffT = at("a_diffT", RD + 71 * K + 1536, [P, 3 * P])
        o_diff = at("o_diff", RD + 74 * K, [P, NT, P])
        junk = at("junk", RD + 60 * K, [P, CW])
        junk_wide = at("junk_wide", RD + 60 * K, [P, D])
        act_hi = at("act_hi", RB, [P, FK, TOK], F32R)
        act_lo = at("act_lo", RB + 44 * K, [P, FK, TOK], F32R)
        up_stage = at("up_stage", RB + 88 * K, [P, NT, CW])
        conv_g = at("conv_g", RB + 92 * K, [P, BPC, TOK])
        conv_v = at("conv_v", RB + 96 * K, [P, BPC, TOK])
        prod = at("prod", RB + 100 * K, [P, BPC, TOK])
        down_junk = at("down_junk", RB + 104 * K, [P, CW])

        PS = ctx.enter_context(nc.psum_tensor("PS", [P, 8, CW], F32))
        ACC = [PS[:, 0:2, :], PS[:, 2:4, :]]
        TURN = PS[:, 4:6, :].rearrange("p b (c t) -> p (b c) t", t=TOK)
        SCORE = PS[:, 6:8, :]
        SCORE_T = PS[:, 6:8, :].rearrange("p b (c t) -> p (b c) t", t=TOK)

        mem_in, x_in, vec_in, lam_in, up_rows_in = (sem(n) for n in ("mem_in", "x_in", "vec_in", "lam_in", "up_rows_in"))
        bias_in, xres_in, gpost_in, glast_in = (sem(n) for n in ("bias_in", "xres_in", "gpost_in", "glast_in"))
        raw_in = [sem(f"raw_in{s}") for s in range(RING)]
        stream_pace = sem("stream_pace")
        norm_pace = sem("norm_pace")
        hi_ready = sem("hi_ready")
        lo_ready = sem("lo_ready")
        block_done = sem("block_done")
        evacuated = [sem("evacuated0"), sem("evacuated1")]
        ident_ready, zero_ready, const_turned, const_ready = (sem(n) for n in ("ident_ready", "zero_ready", "const_turned", "const_ready"))
        prep_turned, prep_hi, prep_lo = (sem(n) for n in ("prep_turned", "prep_hi", "prep_lo"))
        squares = sem("squares")
        rms_ready = sem("rms_ready")
        rms_mean = sem("rms_mean")
        lam_mul, lam_dot, lam_e, lam_ready = (sem(n) for n in ("lam_mul", "lam_dot", "lam_e", "lam_ready"))
        turned_done = sem("turned_done")
        turned_read = sem("turned_read")
        tap0, tap1 = sem("tap0"), sem("tap1")
        yconv_hi, yconv_lo = sem("yconv_hi"), sem("yconv_lo")
        x_scores, x_top, x_exp, x_norm, x_inv = (sem(n) for n in ("x_scores", "x_top", "x_exp", "x_norm", "x_inv"))
        x_pT, x_pT_sb, x_oT, x_hi, x_lo, x_max = (sem(n) for n in ("x_pT", "x_pT_sb", "x_oT", "x_hi", "x_lo", "x_max"))
        d_qk, d_scores, d_mask, d_max, d_top, d_exp = (sem(n) for n in ("d_qk", "d_scores", "d_mask", "d_max", "d_top", "d_exp"))
        d_inv, d_scaled, d_a, d_aT, d_aT_sb, d_o = (sem(n) for n in ("d_inv", "d_scaled", "d_a", "d_aT", "d_aT_sb", "d_o"))
        d_sq, d_ms, d_r, d_on, d_oT, d_hi, d_lo = (sem(n) for n in ("d_sq", "d_ms", "d_r", "d_on", "d_oT", "d_hi", "d_lo"))
        gate_ready, gated_sum, mix_hi = (sem(n) for n in ("gate_ready", "gated_sum", "mix_hi"))
        mix_sq, mix_sum, x_new, h2_sq = (sem(n) for n in ("mix_sq", "mix_sum", "x_new", "h2_sq"))
        silu_done, prod_done, act_hi_done, act_lo_done = (sem(n) for n in ("silu_done", "prod_done", "act_hi_done", "act_lo_done"))
        down_sq, down_y, down_sum, out_ready, out_stored = (sem(n) for n in ("down_sq", "down_y", "down_sum", "out_ready", "out_stored"))

        block = ctx.enter_context(nc.Block())

        def cols(w, k0, c0):
            return w[0, k0 * P:(k0 + KB) * P, bass.ds(c0, CW)].rearrange("(c p) n -> p c n", p=P)

        def down_landed(j, i):
            per_chunk = len(range(i % RING, DB, RING))
            return 4 * N_DN + 16 * (j * per_chunk + i // RING + 1)

        @block.sync
        def _(sp):
            def load(n, i, w, k0, c0):
                if not isinstance(n, int) or n + i >= RING:
                    sp.wait_ge(lo_ready, n + i - RING + 1)
                    if not isinstance(n, int):
                        sp.sem_inc(stream_pace, 1)
                sp.dma_start(raw[i % RING][:], cols(w, k0, c0)).then_inc(raw_in[i % RING], 16)

            for t in range(NT):
                sp.dma_start(mem_sb[:, t, :], mem[0, t * P:(t + 1) * P, :]).then_inc(mem_in, 16)

            for c, (name, half) in enumerate(proj):
                for i in range(CB):
                    if name == "mk":
                        load(c * CB, i, w_mem_kv, i * KB, half * CW)
                    elif name == "mv":
                        load(c * CB, i, w_mem_kv, i * KB, CROSS + half * CW)
                    else:
                        load(c * CB, i, w_in, i * KB, in_cols[name] + half * CW)

            def branch_step(r, j):
                q = NCH * r + j
                n = N_BR + SB * q
                for i in range(CB):
                    load(n, i, w_gate, i * KB, GATE_OF[r] * D + j * CW)
                    if i == 4:
                        sp.wait_ge(evacuated[0], E_BR + q)
                        if not isinstance(q, int):
                            sp.sem_inc(stream_pace, 1)
                        sp.dma_start(bias_bc[:], b_gate[0, bass.ds(GATE_OF[r] * D + j * CW, CW)].partition_broadcast(P)).then_inc(bias_in, 16)
                for i in range(OB):
                    load(n, CB + i, (w_conv_out, w_cross_out, w_diff_out)[r], i * KB, j * CW)

            for r in range(3):
                if r == 1:
                    sp.wait_ge(block_done, N_BR + SB * NCH)
                    for t in range(NT):
                        sp.dma_start(x_res[:, t, :], x[0, t * P:(t + 1) * P, :]).then_inc(xres_in, 16)
                branch_step(r, 0)
                if r == 2:
                    sp.wait_ge(block_done, N_BR + SB * 2 * NCH)
                    sp.dma_start(g_post[:], g_mix_post[0, :].partition_broadcast(P)).then_inc(gpost_in, 16)
                with sp.Fori(1, NCH) as j:
                    branch_step(r, j)
            for j in range(NCH):
                for i in range(CB):
                    load(N_O + j * CB, i, w_o, i * KB, j * CW)
            with sp.Fori(0, NUP) as j:
                for i in range(CB):
                    load(N_UP + 2 * CB * j, i, w_up, i * KB, j * CW)
                for i in range(CB):
                    load(N_UP + 2 * CB * j, CB + i, w_up, i * KB, FF + j * CW)

            def down_chunk(j):
                for i in range(DB):
                    load(N_DN + DBV * j, i, w_down, i * KB, j * CW)
                    if i == 6 and isinstance(j, int):
                        sp.wait_ge(block_done, N_DN)
                        sp.dma_start(g_last[:], g_ffn_post[0, :].partition_broadcast(P)).then_inc(glast_in, 16)

            down_chunk(0)
            with sp.Fori(1, NCH) as j:
                down_chunk(j)
            for g in range(NCH):
                for t in range(NT):
                    if t == 0:
                        sp.wait_ge(out_ready, g + 1)
                    sp.dma_start(out[0, t * P:(t + 1) * P, g * CW:(g + 1) * CW],
                                 y_down[:, t, g * CW:(g + 1) * CW]).then_inc(out_stored, 16)
            sp.wait_ge(out_stored, 16 * NT * NCH)

        @block.gpsimd
        def _(pool):
            nc.gpsimd.memset(ident[:], 0.0).then_inc(zero_ready, 1)
            nc.gpsimd.memset(minus_half[:], -0.5).then_inc(zero_ready, 1)
            pool.wait_ge(zero_ready, 2)
            nc.gpsimd.affine_select(out=ident[:], in_=ident[:], compare_op=ALU.not_equal, fill=1.0, base=0,
                                    pattern=[[-1, P]], channel_multiplier=1).then_inc(ident_ready, 1)
            rms_count = [0]

            def rms(dst, sums, width):
                nc.gpsimd.tensor_scalar(mean_sq[:], sums, 1.0 / width, EPS, ALU.mult, ALU.add).then_inc(rms_mean, 1)
                rms_count[0] += 1
                pool.wait_ge(rms_mean, rms_count[0])
                nc.gpsimd.tensor_tensor(dst, mean_sq[:], minus_half[:], ALU.pow).then_inc(rms_ready, 1)
                pool.wait_ge(rms_ready, rms_count[0])

            pool.wait_ge(squares, 1)
            rms(r_mem[:], sq_mem[:], D)
            pool.wait_ge(squares, 2)
            rms(r_x[:], sq_x[:], D)

            def head(h):
                if not (isinstance(h, int) and h == 0):
                    pool.wait_ge(d_scores, h)
                nc.gpsimd.tensor_copy(qk_head[:, 0, :], qT[:, bass.ds(h, 1), :])
                nc.gpsimd.tensor_copy(qk_head[:, 1, :], kT[:, bass.ds(h, 1), :]).then_inc(d_qk, 1)
                pool.wait_ge(d_sq, h + 1)
                pool.sem_inc(norm_pace, 1)
                nc.gpsimd.tensor_scalar(ms_o[:], sq_o[:], 1.0 / P, EPS, ALU.mult, ALU.add).then_inc(d_ms, 1)
                pool.wait_ge(d_ms, h + 1)
                nc.gpsimd.tensor_tensor(r_o[:], ms_o[:], minus_half[:], ALU.pow).then_inc(d_r, 1)
                pool.wait_ge(d_r, h + 1)

            pool.wait_ge(turned_read, T_MERGE)
            pool.wait_ge(x_lo, CH)
            head(0)
            with pool.Fori(1, DH) as h:
                head(h)

            pool.wait_ge(mix_sum, 1)
            rms(r_mix[:], sq_mix[:], D)
            pool.wait_ge(h2_sq, 1)
            rms(r_h2[:], sq_h2[:], D)
            pool.wait_ge(down_sum, 1)
            rms(r_out[:], sq_down[:], D)

        @block.scalar
        def _(act):
            for dst, src in ((vec_rows[0:DK, :], g_mix_pre[0].rearrange("(b p) -> b p", p=P)),
                             (vec_rows[DK:2 * DK, :], g_mem[0].rearrange("(b p) -> b p", p=P)),
                             (vec_rows[2 * DK:3 * DK, :], g_ffn_pre[0].rearrange("(b p) -> b p", p=P)),
                             (vec_rows[3 * DK:3 * DK + 3 * HK, :], conv_w[0].rearrange("k (b p) -> (k b) p", p=P)),
                             (vec_rows[3 * DK + 3 * HK:3 * DK + 3 * HK + 1, :], g_diff_sub)):
                act.dma_start(dst, src).then_inc(vec_in, 16)
            act.dma_start(up_rows[0:2 * FK, :, :], ffn_conv_w[0].rearrange("k (b p) -> b k p", p=P)).then_inc(up_rows_in, 16)
            for n, l in enumerate((lambda_q1, lambda_k1, lambda_q2, lambda_k2)):
                act.dma_start(lam_rows[:, n, :], l[0].partition_broadcast(P)).then_inc(lam_in, 16)
            for t in range(NT):
                act.dma_start(x_sb[:, t, :], x[0, t * P:(t + 1) * P, :]).then_inc(x_in, 16)

            def split(n, i, landed=None, inc=1):
                act.wait_ge(raw_in[i % RING], 4 * n + 16 * (i // RING + 1) if landed is None else landed)
                if not isinstance(n, int) or n + i >= RING:
                    act.wait_ge(block_done, n + i - RING + 1)
                nc.scalar.activation(w_hi[i % RING][:], raw[i % RING][:], ACT.Copy).then_inc(hi_ready, inc)

            def prepare(G, g, src, gains, dst):
                act.wait_ge(prep_turned, G + 1)
                for b in range(BPC):
                    last = nc.scalar.activation(dst[:, BPC * g + b, :], src[:, b, :], ACT.Copy,
                                                scale=gains[:, BPC * g + b:BPC * g + b + 1])
                last.then_inc(prep_hi, 1)

            act.wait_ge(const_ready, 2)
            for g in range(NCH):
                prepare(g, g, (TURN, SCORE_T)[g % 2], g_mem_v, memT_hi)
            act.wait_ge(mem_in, 16 * NT)
            for t in range(NT):
                last = nc.scalar.activation(junk_wide[:], mem_sb[:, t, :], ACT.Square, accum_out=sq_mem[:, t:t + 1])
                if t == 0:
                    last.then_inc(junk_free := sem("junk_free"), 1)
                    act.wait_ge(junk_free, 1)
            last.then_inc(squares, 1)
            act.wait_ge(squares, 1)

            def evacuate(c, n_end, dst, scale, wait=None):
                act.wait_ge(block_done, n_end)
                for t in range(NT):
                    last = nc.scalar.activation(dst[:, t, :], ACC[c % 2][:, t, :], ACT.Copy, scale=scale[:, t:t + 1])
                last.then_inc(evacuated[c % 2], 1)

            def after_projection(c):
                name, half = proj[c]
                s = slice(half * CW, (half + 1) * CW)
                n_end = (c + 1) * CB
                if c == 0:
                    act.wait_ge(rms_ready, 1)
                if c == 4:
                    act.wait_ge(rms_ready, 2)
                if name == "mv":
                    evacuate(c, n_end, mv_tok[:, :, s], r_mem)
                elif name == "dv":
                    evacuate(c, n_end, v_tok[:, :, s], r_x)
                elif name == "cc":
                    if half:
                        act.wait_ge(evacuated[(c - 1) % 2], (c - 1) // 2 + 1)
                    evacuate(c, n_end, cc_sb, r_x)
                elif name != "cv":
                    if TI[proj[c]]:
                        act.wait_ge(turned_done, TI[proj[c]])
                    evacuate(c, n_end, stage, r_mem if name == "mk" else r_x)

            def first_tap(k, dst, taps):
                act.wait_ge(turned_done, k + 1)
                for b in range(BPC):
                    last = nc.scalar.activation(dst[:, b, :], TURN[:, b, :], ACT.Copy, scale=taps[b])
                last.then_inc(tap0, 1)

            def cross_exp(h):
                act.wait_ge(x_top, h + 1)
                for t in range(NT):
                    last = nc.scalar.activation(p_cross[:, t, :], PS[:, 6, t * TOK:(t + 1) * TOK], ACT.Exp,
                                                bias=neg_top[:, 0, t:t + 1], scale=CHD ** -0.5,
                                                accum_out=psum_e[:, 0, t:t + 1])
                last.then_inc(x_exp, 1)

            for c, (name, half) in enumerate(proj):
                for i in range(CB):
                    split(c * CB, i)
                    if i == 2 and c:
                        after_projection(c - 1)
                    if c < NCH and i == 6:
                        prepare(NCH + c, c, SCORE_T, g_pre_v, hT_hi)
                    if c == 0 and i == 7:
                        act.wait_ge(x_in, 16 * NT)
                        for t in range(NT):
                            last = nc.scalar.activation(junk_wide[:], x_sb[:, t, :], ACT.Square, accum_out=sq_x[:, t:t + 1])
                            if t == 0:
                                last.then_inc(junk_free, 1)
                                act.wait_ge(junk_free, 2)
                        last.then_inc(squares, 1)
                        act.wait_ge(lam_dot, 1)
                        nc.scalar.activation(lam_exp[:], lam_dots[:], ACT.Exp).then_inc(lam_e, 1)
                    if i == 5 and c and proj[c - 1][0] == "cv":
                        hp = proj[c - 1][1]
                        first_tap(TI[proj[c - 1]], convT[:, BPC * hp:BPC * (hp + 1), :],
                                  [taps_v[:, 2 * HK + BPC * hp + b:2 * HK + BPC * hp + b + 1] for b in range(BPC)])
                    if i == 6 and c and proj[c - 1][0] == "cb":
                        hp = proj[c - 1][1]
                        act.wait_ge(turned_read, TI[proj[c - 1]] + 1)
                        nc.scalar.activation(y_conv_hi[:, BPC * hp:BPC * (hp + 1), :], y_tmp[:], ACT.Copy).then_inc(yconv_hi, 1)
                    h = c - CROSS_STEP
                    if 0 <= h < CH:
                        if i == 3:
                            cross_exp(h)
                        if i == 6:
                            act.wait_ge(x_pT, h + 1)
                            nc.scalar.activation(p_crossT[:], PS[:, 7, :].rearrange("p (a b) -> p a b", a=NT), ACT.Copy).then_inc(x_pT_sb, 1)
                        if i == 7:
                            act.wait_ge(x_oT, h + 1)
                            nc.scalar.activation(y_cross_hi[:, 2 * h:2 * h + 2, :],
                                                 PS[:, 6, :].rearrange("p (a b) -> p a b", a=2), ACT.Copy).then_inc(x_hi, 1)

            def merge_hi(j):
                act.wait_ge(turned_done, T_MERGE + j + 1)
                nc.scalar.activation(mixT_hi[:, bass.ds(BPC * j, BPC), :], TURN, ACT.Copy, scale=0.5).then_inc(mix_hi, 1)

            def branch_step(r, j, jp):
                q = NCH * r + j
                n = N_BR + SB * q
                for i in range(SB):
                    split(n, i)
                    if i == 2 and isinstance(q, int) and q == 0:
                        after_projection(NP - 1)
                    if i == 5 and r == 2 and jp is not None:
                        merge_hi(jp)
                    if r < 2:
                        if i == 3:
                            act.wait_ge(d_top, q + 1)
                            for t, (s0, s1) in enumerate(((0, P), (P, 3 * P))):
                                for m in range(2):
                                    last = nc.scalar.activation(p_diff[:, m, s0:s1], SCORE[:, m, s0:s1], ACT.Exp,
                                                                bias=neg_top[:, t, m:m + 1], scale=DQK ** -0.5,
                                                                accum_out=psum_e[:, t, m:m + 1])
                            last.then_inc(d_exp, 1)
                        if i == 5:
                            act.wait_ge(d_aT, q + 1)
                            nc.scalar.activation(a_diffT[:], PS[:, 4, 0:3 * P], ACT.Copy).then_inc(d_aT_sb, 1)
                        if i == 7:
                            act.wait_ge(d_o, q + 1)
                            for t in range(NT):
                                last = nc.scalar.activation(o_diff[:, t, :], PS[:, 5, t * P:(t + 1) * P], ACT.Square,
                                                            accum_out=sq_o[:, t:t + 1])
                            last.then_inc(d_sq, 1)
                        if i == 9:
                            act.wait_ge(d_oT, q + 1)
                            nc.scalar.activation(y_diff_hi[:, bass.ds(q, 1), :], PS[:, 4, 0:TOK].rearrange("p (a t) -> p a t", a=1), ACT.Copy,
                                                 scale=g_sub[:, 0:1]).then_inc(d_hi, 1)
                    if i == 10:
                        act.wait_ge(evacuated[0], E_BR + q + 1)
                        act.wait_ge(evacuated[1], E_BR + q)
                        nc.scalar.activation(gate_tanh[:], gate_pre[:], ACT.Tanh, scale=0.5).then_inc(gate_ready, 1)

            for r in range(3):
                branch_step(r, 0, None)
                with act.Fori(1, NCH) as j:
                    branch_step(r, j, j - 1)

            def mix_squares(c):
                act.wait_ge(block_done, N_O + CB * (c + 1))
                for t in range(NT):
                    if c or t:
                        act.wait_ge(mix_sq, NT * c + t)
                    nc.scalar.activation(junk[:], ACC[c % 2][:, t, :], ACT.Square,
                                         accum_out=sq_part[:, t, c:c + 1]).then_inc(mix_sq, 1)

            for c in range(NCH):
                for i in range(CB):
                    split(N_O + CB * c, i)
                    if i == 2 and c:
                        mix_squares(c - 1)
                    if i == 5 and c == 0:
                        merge_hi(NCH - 1)

            def up_evacuate(k, n_end, parity):
                act.wait_ge(turned_done, k)
                act.wait_ge(block_done, n_end)
                for t in range(NT):
                    last = nc.scalar.activation(up_stage[:, t, :], ACC[parity][:, t, :], ACT.Copy, scale=r_h2[:, t:t + 1])
                last.then_inc(evacuated[parity], 1)

            def up_first_tap(k, dst, blk):
                act.wait_ge(turned_done, k + 1)
                for b in range(BPC):
                    last = nc.scalar.activation(dst[:, b, :], TURN[:, b, :], ACT.Copy, scale=up_taps[:, 2, bass.ds(blk + b, 1)])
                last.then_inc(tap0, 1)

            def value_done(j, i):
                if i == 2:
                    up_evacuate(T_UP + 2 * j + 1, N_UP + 2 * CB * j + 2 * CB, 1)
                if i == 5:
                    if not (isinstance(j, int) and j == 0):
                        act.wait_ge(prod_done, j)
                    up_first_tap(T_UP + 2 * j + 1, conv_v, FK + BPC * j)
                if i == 7:
                    act.wait_ge(prod_done, j + 1)
                    nc.scalar.activation(act_hi[:, bass.ds(BPC * j, BPC), :], prod[:], ACT.Copy).then_inc(act_hi_done, 1)

            def up_step(j, jp):
                n = N_UP + 2 * CB * j
                for i in range(CB):
                    split(n, i)
                    if jp is not None:
                        value_done(jp, i)
                    elif i == 2:
                        mix_squares(NCH - 1)
                        for g in range(NCH):
                            prepare(2 * NCH + g, g, (SCORE_T, TURN)[g % 2], g_ffn_v, h2_hi)
                        for t in range(NT):
                            act.wait_ge(h2_free := mix_sq, NT * NCH + t)
                            last = nc.scalar.activation(junk_wide[:], x_res[:, t, :], ACT.Square, accum_out=sq_h2[:, t:t + 1])
                            last.then_inc(mix_sq, 1)
                        act.wait_ge(mix_sq, NT * NCH + NT)
                for i in range(CB):
                    split(n, CB + i)
                    if i == 2:
                        if jp is None:
                            act.wait_ge(rms_ready, 4)
                        up_evacuate(T_UP + 2 * j, n + CB, 0)
                    if i == 5:
                        if jp is not None:
                            act.wait_ge(prod_done, j)
                        up_first_tap(T_UP + 2 * j, conv_g, BPC * j)
                    if i == 6:
                        act.wait_ge(turned_read, T_UP + 2 * j + 1)
                        nc.scalar.activation(conv_g[:], conv_g[:], ACT.Silu).then_inc(silu_done, 1)

            up_step(0, None)
            with act.Fori(1, NUP) as j:
                up_step(j, j - 1)

            def down_squares(jp):
                act.wait_ge(block_done, N_DN + DBV * (jp + 1))
                for t in range(NT):
                    act.wait_ge(down_sq, NT * jp + t)
                    nc.scalar.activation(down_junk[:], PS[:, bass.ds(NT * jp + t, 1), :].rearrange("p a n -> p (a n)"), ACT.Square,
                                         accum_out=sq_part2[:, t, bass.ds(jp, 1)]).then_inc(down_sq, 1)

            def down_chunk(j, jp):
                for i in range(DB):
                    split(N_DN + DBV * j, i, down_landed(j, i), 1 if i < DB - 1 else 1 + DBV - DB)
                    if jp is None:
                        value_done(NUP - 1, i)
                    elif i == 2:
                        down_squares(jp)

            down_chunk(0, None)
            with act.Fori(1, NCH) as j:
                down_chunk(j, j - 1)
            down_squares(NCH - 1)

        @block.vector
        def _(dve):
            def split(n, i, inc=1):
                dve.wait_ge(hi_ready, n + i + 1)
                nc.vector.tensor_tensor(w_lo[i % RING][:], raw[i % RING][:], w_hi[i % RING][:].bitcast(F32),
                                        ALU.subtract).then_inc(lo_ready, inc)

            def prepare(G, g, src, gains, hi, lo):
                dve.wait_ge(prep_hi, G + 1)
                for b in range(BPC):
                    kb = BPC * g + b
                    last = nc.vector.scalar_tensor_tensor(out=lo[:, kb, :], in0=src[:, b, :], scalar=gains[:, kb:kb + 1],
                                                          in1=hi[:, kb, :].bitcast(F32), op0=ALU.mult, op1=ALU.subtract)
                last.then_inc(prep_lo, 1)

            dve.wait_ge(const_turned, 1)
            nc.vector.tensor_copy(vecs[:], PS[:, 0, 0:3 * DK + 3 * HK + 1]).then_inc(const_ready, 1)
            nc.vector.tensor_copy(up_taps[:], PS[:, 1, 0:6 * FK].rearrange("p (k b) -> p k b", k=3)).then_inc(const_ready, 1)
            dve.wait_ge(const_ready, 2)
            nc.vector.tensor_scalar(g_sub[:], vecs[:, 3 * DK + 3 * HK:3 * DK + 3 * HK + 1], 1.0 - LAMBDA_INIT, None,
                                    ALU.mult).then_inc(const_ready, 1)
            for g in range(NCH):
                prepare(g, g, (TURN, SCORE_T)[g % 2], g_mem_v, memT_hi, memT_lo)
            dve.wait_ge(lam_in, 64)
            nc.vector.tensor_tensor(lam_prod[:], lam_rows[:, 0:4:2, :], lam_rows[:, 1:4:2, :], ALU.mult).then_inc(lam_mul, 1)
            dve.wait_ge(lam_mul, 1)
            nc.vector.tensor_reduce(lam_dots[:], lam_prod[:], AX.X, ALU.add).then_inc(lam_dot, 1)

            def turned_conv(k, dst, taps):
                dve.wait_ge(tap0, conv_count(k) + 1)
                for b in range(BPC):
                    last = nc.vector.scalar_tensor_tensor(out=dst[:, b, 1:TOK], in0=TURN[:, b, 0:TOK - 1], scalar=taps(1, b),
                                                          in1=dst[:, b, 1:TOK], op0=ALU.mult, op1=ALU.add)
                last.then_inc(tap1, 1)
                dve.wait_ge(tap1, conv_count(k) + 1)
                for b in range(BPC):
                    last = nc.vector.scalar_tensor_tensor(out=dst[:, b, 2:TOK], in0=TURN[:, b, 0:TOK - 2], scalar=taps(0, b),
                                                          in1=dst[:, b, 2:TOK], op0=ALU.mult, op1=ALU.add)
                last.then_inc(turned_read, 1)

            def conv_count(k):
                if isinstance(k, int) and k < T_UP:
                    return [TI[("cv", 0)], TI[("cv", 1)]].index(k)
                return k - T_UP + 2

            def after_projection(c, i):
                name, half = proj[c]
                k = TI.get(proj[c])
                s = slice(half * BPC, (half + 1) * BPC)
                if i == 2 and name == "cv":
                    dve.wait_ge(turned_done, k)
                    dve.wait_ge(evacuated[(c - 1) % 2], (c - 1) // 2 + 1)
                    dve.wait_ge(block_done, (c + 1) * CB)
                    for t in range(NT):
                        last = nc.vector.scalar_tensor_tensor(out=stage[:, t, :], in0=ACC[c % 2][:, t, :], scalar=r_x[:, t:t + 1],
                                                              in1=cc_sb[:, t, :], op0=ALU.mult, op1=ALU.mult)
                    last.then_inc(evacuated[c % 2], 1)
                if i == 5 and name == "cv":
                    turned_conv(k, convT[:, s, :], lambda m, b: taps_v[:, m * HK + half * BPC + b:m * HK + half * BPC + b + 1])
                if i == 5 and name in ("mk", "xq", "dq", "dk"):
                    dve.wait_ge(turned_done, k + 1)
                    dst = {"mk": mkT, "xq": xqT, "dq": qT, "dk": kT}[name]
                    nc.vector.tensor_copy(dst[:, s, :], TURN).then_inc(turned_read, 1)
                if i == 5 and name == "cb":
                    dve.wait_ge(turned_done, k + 1)
                    if half == 0:
                        dve.wait_ge(turned_read, TI[("cv", 1)] + 1)
                    else:
                        dve.wait_ge(yconv_lo, 1)
                    nc.vector.tensor_tensor(y_tmp[:], TURN, convT[:, s, :], ALU.mult).then_inc(turned_read, 1)
                if i == 6 and name == "cb":
                    dve.wait_ge(yconv_hi, half + 1)
                    nc.vector.tensor_tensor(y_conv_lo[:, s, :], y_tmp[:], y_conv_hi[:, s, :].bitcast(F32),
                                            ALU.subtract).then_inc(yconv_lo, 1)

            for c, (name, half) in enumerate(proj):
                for i in range(CB):
                    split(c * CB, i)
                    if c:
                        after_projection(c - 1, i)
                    if c < NCH and i == 6:
                        prepare(NCH + c, c, SCORE_T, g_pre_v, hT_hi, hT_lo)
                    if c == 1 and i == 0:
                        dve.wait_ge(lam_e, 1)
                        nc.vector.scalar_tensor_tensor(out=minus_lam[:], in0=lam_exp[:, 1:2], scalar=LAMBDA_INIT, in1=lam_exp[:, 0:1],
                                                       op0=ALU.subtract, op1=ALU.subtract).then_inc(lam_ready, 1)
                    h = c - CROSS_STEP
                    if 0 <= h < CH:
                        if i == 3:
                            dve.wait_ge(x_scores, h + 1)
                            if h:
                                dve.wait_ge(x_exp, h)
                            nc.vector.tensor_reduce(top[:, 0, :], PS[:, 6, :].rearrange("p (t k) -> p t k", t=NT), AX.X,
                                                    ALU.max).then_inc(x_max, 1)
                            dve.wait_ge(x_max, h + 1)
                            nc.vector.tensor_scalar(neg_top[:, 0, :], top[:, 0, :], -CHD ** -0.5, None, ALU.mult).then_inc(x_top, 1)
                        if i == 4:
                            dve.wait_ge(x_exp, h + 1)
                            nc.vector.reciprocal(inv_e[:, 0, :], psum_e[:, 0, :]).then_inc(x_inv, 1)
                            dve.wait_ge(x_inv, h + 1)
                            for t in range(NT):
                                last = nc.vector.tensor_scalar(p_cross[:, t, :], p_cross[:, t, :], inv_e[:, 0, t:t + 1], None, ALU.mult)
                            last.then_inc(x_norm, 1)
                        if i == 7:
                            dve.wait_ge(x_hi, h + 1)
                            nc.vector.tensor_tensor(y_cross_lo[:, 2 * h:2 * h + 2, :], PS[:, 6, :].rearrange("p (a b) -> p a b", a=2),
                                                    y_cross_hi[:, 2 * h:2 * h + 2, :].bitcast(F32), ALU.subtract).then_inc(x_lo, 1)

            def gate_product(r, jp, q_prev):
                dve.wait_ge(block_done, N_BR + SB * (q_prev + 1))
                dve.wait_ge(gate_ready, q_prev + 1)
                first = r == 0
                if r == 1 and isinstance(jp, int) and jp == 0:
                    dve.wait_ge(evacuated[1], E_BR + NCH)
                if r == 2 or not first:
                    pass
                for t in range(NT):
                    dst = merged[:, t, bass.ds(jp * CW, CW)] if first else gated[:, t, :]
                    last = nc.vector.scalar_tensor_tensor(out=dst, in0=gate_tanh[:, t, :], scalar=1.0, in1=ACC[1][:, t, :],
                                                          op0=ALU.add, op1=ALU.mult)
                last.then_inc(evacuated[1], 1)
                if not first:
                    dve.wait_ge(evacuated[1], E_BR + q_prev + 1)
                    m = merged[:, :, bass.ds(jp * CW, CW)]
                    if r == 2:
                        dve.wait_ge(turned_done, T_MERGE + jp)
                    nc.vector.tensor_tensor(m if r == 1 else stage[:], m, gated[:], ALU.add).then_inc(gated_sum, 1)
                    dve.wait_ge(gated_sum, q_prev - NCH + 1)

            def merge_lo(j):
                dve.wait_ge(mix_hi, j + 1)
                nc.vector.scalar_tensor_tensor(out=mixT_lo[:, bass.ds(BPC * j, BPC), :].rearrange("p a t -> p (a t)"),
                                               in0=TURN.rearrange("p a t -> p (a t)"), scalar=0.5,
                                               in1=mixT_hi[:, bass.ds(BPC * j, BPC), :].bitcast(F32).rearrange("p a t -> p (a t)"),
                                               op0=ALU.mult, op1=ALU.subtract).then_inc(turned_read, 1)

            def branch_step(r, j, rp, jp):
                q = NCH * r + j
                n = N_BR + SB * q
                for i in range(SB):
                    split(n, i)
                    if i == 2 and rp is not None:
                        gate_product(rp, jp, q - 1)
                    if i == 5 and rp == 2:
                        merge_lo(jp)
                    if r < 2:
                        if i == 3:
                            dve.wait_ge(d_scores, q + 1)
                            nc.vector.memset(SCORE[0:64, :, 64:128], -1e37)
                            nc.vector.memset(SCORE[0:64, :, 320:384], -1e37).then_inc(d_mask, 1)
                            dve.wait_ge(d_mask, q + 1)
                            nc.vector.tensor_reduce(top[:, 0, :], SCORE[:, :, 0:P], AX.X, ALU.max)
                            nc.vector.tensor_reduce(top[:, 1, :], SCORE[:, :, P:3 * P], AX.X, ALU.max).then_inc(d_max, 1)
                            dve.wait_ge(d_max, q + 1)
                            nc.vector.tensor_scalar(neg_top[:], top[:], -DQK ** -0.5, None, ALU.mult).then_inc(d_top, 1)
                        if i == 4:
                            dve.wait_ge(d_exp, q + 1)
                            nc.vector.reciprocal(inv_e[:], psum_e[:]).then_inc(d_inv, 1)
                            dve.wait_ge(d_inv, 2 * q + 1)
                            nc.vector.tensor_scalar(lam_inv[:], inv_e[:, :, 1], minus_lam[:, 0:1], None, ALU.mult).then_inc(d_inv, 1)
                            dve.wait_ge(d_inv, 2 * q + 2)
                            for t, (s0, s1) in enumerate(((0, P), (P, 3 * P))):
                                last = nc.vector.tensor_scalar(p_diff[:, 1, s0:s1], p_diff[:, 1, s0:s1], lam_inv[:, t:t + 1], None, ALU.mult)
                            last.then_inc(d_scaled, 1)
                            dve.wait_ge(d_scaled, q + 1)
                            for t, (s0, s1) in enumerate(((0, P), (P, 3 * P))):
                                last = nc.vector.scalar_tensor_tensor(out=a_diff[:, s0:s1], in0=p_diff[:, 0, s0:s1], scalar=inv_e[:, t, 0:1],
                                                                      in1=p_diff[:, 1, s0:s1], op0=ALU.mult, op1=ALU.add)
                            last.then_inc(d_a, 1)
                        if i == 8:
                            dve.wait_ge(d_r, q + 1)
                            for t in range(NT):
                                last = nc.vector.tensor_scalar(o_diff[:, t, :], PS[:, 5, t * P:(t + 1) * P], r_o[:, t:t + 1], None, ALU.mult)
                            last.then_inc(d_on, 1)
                        if i == 9:
                            dve.wait_ge(d_hi, q + 1)
                            nc.vector.scalar_tensor_tensor(out=y_diff_lo[:, bass.ds(q, 1), :].rearrange("p a t -> p (a t)"), in0=PS[:, 4, 0:TOK],
                                                           scalar=g_sub[:, 0:1],
                                                           in1=y_diff_hi[:, bass.ds(q, 1), :].bitcast(F32).rearrange("p a t -> p (a t)"),
                                                           op0=ALU.mult, op1=ALU.subtract).then_inc(d_lo, 1)
                    if i == 10:
                        dve.wait_ge(block_done, n + CB)
                        dve.wait_ge(bias_in, 16 * (q + 1))
                        if rp is not None:
                            dve.wait_ge(gate_ready, q)
                        for t in range(NT):
                            last = nc.vector.scalar_tensor_tensor(out=gate_pre[:, t, :], in0=ACC[0][:, t, :], scalar=r_x[:, t:t + 1],
                                                                  in1=bias_bc[:], op0=ALU.mult, op1=ALU.add)
                        last.then_inc(evacuated[0], 1)

            dve.wait_ge(lam_ready, 1)
            dve.wait_ge(const_ready, 3)
            for r in range(3):
                branch_step(r, 0, r - 1 if r else None, NCH - 1)
                with dve.Fori(1, NCH) as j:
                    branch_step(r, j, r, j - 1)

            def mix_out(c):
                if c == 0:
                    dve.wait_ge(gpost_in, 16)
                dve.wait_ge(mix_sq, NT * (c + 1))
                for t in range(NT):
                    s = slice(c * CW, (c + 1) * CW)
                    last = nc.vector.tensor_tensor(y_mix[:, t, s], ACC[c % 2][:, t, :], g_post[:, s], ALU.mult)
                last.then_inc(evacuated[c % 2], 1)

            for c in range(NCH):
                for i in range(CB):
                    split(N_O + CB * c, i)
                    if i == 2:
                        if c:
                            mix_out(c - 1)
                        else:
                            gate_product(2, NCH - 1, 3 * NCH - 1)
                    if i == 5 and c == 0:
                        merge_lo(NCH - 1)

            def value_done(j, i):
                if i == 5:
                    turned_conv(T_UP + 2 * j + 1, conv_v, lambda m, b: up_taps[:, m, bass.ds(FK + BPC * j + b, 1)])
                if i == 6:
                    dve.wait_ge(turned_read, T_UP + 2 * j + 2)
                    dve.wait_ge(silu_done, j + 1)
                    if not (isinstance(j, int) and j == 0):
                        dve.wait_ge(act_lo_done, j)
                    nc.vector.tensor_tensor(prod[:], conv_g[:], conv_v[:], ALU.mult).then_inc(prod_done, 1)
                if i == 7:
                    dve.wait_ge(act_hi_done, j + 1)
                    nc.vector.tensor_tensor(act_lo[:, bass.ds(BPC * j, BPC), :], prod[:],
                                            act_hi[:, bass.ds(BPC * j, BPC), :].bitcast(F32), ALU.subtract).then_inc(act_lo_done, 1)

            def new_x():
                mix_out(NCH - 1)
                nc.vector.tensor_reduce(sq_mix[:], sq_part[:], AX.X, ALU.add).then_inc(mix_sum, 1)
                dve.wait_ge(evacuated[1], E_UP)
                dve.wait_ge(evacuated[0], E_UP)
                dve.wait_ge(xres_in, 16 * NT)
                dve.wait_ge(rms_ready, 3)
                for g in range(NCH + 1):
                    if g < NCH:
                        s = slice(g * CW, (g + 1) * CW)
                        for t in range(NT):
                            last = nc.vector.scalar_tensor_tensor(out=x_res[:, t, s], in0=y_mix[:, t, s], scalar=r_mix[:, t:t + 1],
                                                                  in1=x_res[:, t, s], op0=ALU.mult, op1=ALU.add)
                        last.then_inc(x_new, 1)
                    if g:
                        prepare(2 * NCH + g - 1, g - 1, (SCORE_T, TURN)[(g - 1) % 2], g_ffn_v, h2_hi, h2_lo)
                dve.wait_ge(mix_sq, NT * NCH + NT)
                nc.vector.tensor_copy(sq_mix[:], sq_h2[:]).then_inc(h2_sq, 1)

            def up_step(j, jp):
                n = N_UP + 2 * CB * j
                for i in range(CB):
                    split(n, i)
                    if jp is not None:
                        value_done(jp, i)
                    elif i == 2:
                        new_x()
                for i in range(CB):
                    split(n, CB + i)
                    if i == 5:
                        turned_conv(T_UP + 2 * j, conv_g, lambda m, b: up_taps[:, m, bass.ds(BPC * j + b, 1)])

            up_step(0, None)
            with dve.Fori(1, NUP) as j:
                up_step(j, j - 1)

            def down_out(jp):
                dve.wait_ge(down_sq, NT * (jp + 1))
                for t in range(NT):
                    last = nc.vector.tensor_tensor(y_down[:, t, bass.ds(jp * CW, CW)],
                                                   PS[:, bass.ds(NT * jp + t, 1), :].rearrange("p a n -> p (a n)"),
                                                   g_last[:, bass.ds(jp * CW, CW)], ALU.mult)
                last.then_inc(down_y, 1)

            def down_chunk(j, jp):
                for i in range(DB):
                    split(N_DN + DBV * j, i, 1 if i < DB - 1 else 1 + DBV - DB)
                    if jp is None:
                        value_done(NUP - 1, i)
                    elif i == 2:
                        down_out(jp)

            down_chunk(0, None)
            dve.wait_ge(glast_in, 16)
            with dve.Fori(1, NCH) as j:
                down_chunk(j, j - 1)
            dve.wait_ge(down_sq, NT * NCH)
            nc.vector.tensor_reduce(sq_down[:], sq_part2[:], AX.X, ALU.add).then_inc(down_sum, 1)
            down_out(NCH - 1)
            dve.wait_ge(down_y, NCH)
            dve.wait_ge(rms_ready, 5)
            for g in range(NCH):
                s = slice(g * CW, (g + 1) * CW)
                for t in range(NT):
                    last = nc.vector.scalar_tensor_tensor(out=y_down[:, t, s], in0=y_down[:, t, s], scalar=r_out[:, t:t + 1],
                                                          in1=x_res[:, t, s], op0=ALU.mult, op1=ALU.add)
                last.then_inc(out_ready, 1)

        @block.tensor
        def _(pe):
            def multiply(n, i, nblk, hi, lo, acc, inc=1):
                pe.wait_ge(lo_ready, n + i + 1)
                for c in range(KB):
                    k = KB * i + c
                    first, last_k = k == 0, k == KB * nblk - 1
                    for t in range(NT):
                        s = slice(t * P, (t + 1) * P)
                        o = acc(t)
                        a_hi, a_lo, b_hi, b_lo = hi[:, k, s], lo[:, k, s], w_hi[i % RING][:, c, :], w_lo[i % RING][:, c, :]
                        nc.tensor.matmul(o, a_hi, b_hi, start=first, stop=False)
                        nc.tensor.matmul(o, a_hi, b_lo, start=False, stop=False)
                        last = nc.tensor.matmul(o, a_lo, b_hi, start=False, stop=last_k)
                last.then_inc(block_done, inc)

            def turn(src, dst, signal):
                for t in range(NT):
                    for b in range(BPC):
                        last = nc.tensor.transpose(dst[:, b, t * P:(t + 1) * P], src[:, t, b * P:(b + 1) * P], ident[:])
                last.then_inc(signal, 1)

            NV = 3 * DK + 3 * HK + 1
            pe.wait_ge(ident_ready, 1)
            pe.wait_ge(vec_in, 80)
            pe.wait_ge(up_rows_in, 16)
            nc.tensor.transpose(PS[:, 0, 0:NV], vec_rows[0:NV, :], ident[0:NV, 0:NV])
            for k in range(3):
                last = nc.tensor.transpose(PS[:, 1, k * 2 * FK:(k + 1) * 2 * FK], up_rows[0:2 * FK, k, :], ident[0:2 * FK, 0:2 * FK])
            last.then_inc(const_turned, 1)
            pe.wait_ge(mem_in, 16 * NT)
            for g in range(NCH):
                if g >= 2:
                    pe.wait_ge(prep_lo, g - 1)
                turn(mem_sb[:, :, g * CW:(g + 1) * CW], (TURN, SCORE_T)[g % 2], prep_turned)

            for c, (name, half) in enumerate(proj):
                acc = ACC[c % 2]
                if c >= 2:
                    pe.wait_ge(evacuated[c % 2], c // 2)
                else:
                    pe.wait_ge(const_ready, 2)
                on_mem = name in ("mk", "mv")
                for i in range(CB):
                    if c == 0 or c == NCH:
                        pe.wait_ge(prep_lo, (0 if c == 0 else NCH) + i // 2 + 1)
                    multiply(c * CB, i, CB, memT_hi if on_mem else hT_hi, memT_lo if on_mem else hT_lo, lambda t: acc[:, t, :])
                    if i == 1 and c and proj[c - 1] in TI:
                        k = TI[proj[c - 1]]
                        pe.wait_ge(evacuated[(c - 1) % 2], (c - 1) // 2 + 1)
                        if k:
                            pe.wait_ge(turned_read, k)
                        turn(stage, TURN, turned_done)
                    if c < NCH and i == 3:
                        pe.wait_ge(x_in, 16 * NT)
                        pe.wait_ge(prep_lo, NCH + c)
                        turn(x_sb[:, :, c * CW:(c + 1) * CW], SCORE_T, prep_turned)
                    h = c - CROSS_STEP
                    if 0 <= h < CH:
                        if i == 0:
                            if h:
                                pe.wait_ge(x_lo, h)
                            pe.wait_ge(turned_read, TI[("xq", 1)] + 1)
                            for t in range(NT):
                                for kk in range(2):
                                    last = nc.tensor.matmul(PS[:, 6, t * TOK:(t + 1) * TOK], xqT[:, 2 * h + kk, t * P:(t + 1) * P],
                                                            mkT[:, 2 * h + kk, :], start=kk == 0, stop=kk == 1)
                            last.then_inc(x_scores, 1)
                        if i == 2:
                            pe.wait_ge(x_norm, h + 1)
                            for kb in range(NT):
                                for t in range(NT):
                                    last = nc.tensor.transpose(PS[:, 7, kb * TOK + t * P:kb * TOK + (t + 1) * P],
                                                               p_cross[:, t, kb * P:(kb + 1) * P], ident[:])
                            last.then_inc(x_pT, 1)
                        if i == 4:
                            pe.wait_ge(x_pT_sb, h + 1)
                            for db in range(2):
                                for kb in range(NT):
                                    v0 = h * CHD + db * P
                                    last = nc.tensor.matmul(PS[:, 6, db * TOK:(db + 1) * TOK], mv_tok[:, kb, v0:v0 + P],
                                                            p_crossT[:, kb, :], start=kb == 0, stop=kb == NT - 1)
                            last.then_inc(x_oT, 1)

            def turn_merged(k):
                pe.wait_ge(gated_sum, k - T_MERGE + NCH + 1)
                pe.wait_ge(turned_read, k)
                turn(stage, TURN, turned_done)

            def branch_step(r, j, jp):
                q = NCH * r + j
                n = N_BR + SB * q
                pe.wait_ge(evacuated[0], E_BR + q)
                for i in range(SB):
                    if i < CB:
                        multiply(n, i, CB, hT_hi, hT_lo, lambda t: ACC[0][:, t, :])
                    else:
                        if i == CB:
                            pe.wait_ge(evacuated[1], E_BR + q)
                            pe.wait_ge(*((yconv_lo, 2), (x_lo, CH), (d_lo, DH))[r])
                        y_hi, y_lo = ((y_conv_hi, y_conv_lo), (y_cross_hi, y_cross_lo), (y_diff_hi, y_diff_lo))[r]
                        multiply_out(n, i, y_hi, y_lo)
                    if i == 1 and r == 2 and jp is not None:
                        turn_merged(T_MERGE + jp)
                    if r < 2:
                        if i == 0:
                            pe.wait_ge(d_qk, q + 1)
                            for m in range(2):
                                s = slice(m * DQK, (m + 1) * DQK)
                                nc.tensor.matmul(PS[:, 6 + m, 0:P], qk_head[s, 0, 0:P], qk_head[s, 1, 0:P], start=True, stop=True)
                                last = nc.tensor.matmul(PS[:, 6 + m, P:3 * P], qk_head[s, 0, P:2 * P], qk_head[s, 1, :], start=True, stop=True)
                            last.then_inc(d_scores, 1)
                        if i == 2:
                            pe.wait_ge(d_a, q + 1)
                            for b in range(3):
                                last = nc.tensor.transpose(PS[:, 4, b * P:(b + 1) * P], a_diff[:, b * P:(b + 1) * P], ident[:])
                            last.then_inc(d_aT, 1)
                        if i == 4:
                            pe.wait_ge(d_aT_sb, q + 1)
                            v0, v1 = (v_tok[:, kb, bass.ds(q * P, P)] for kb in range(2))
                            nc.tensor.matmul(PS[:, 5, 0:P], a_diffT[:, 0:P], v0, start=True, stop=True)
                            nc.tensor.matmul(PS[:, 5, P:2 * P], a_diffT[:, P:2 * P], v0, start=True, stop=False)
                            nc.tensor.matmul(PS[:, 5, P:2 * P], a_diffT[:, 2 * P:3 * P], v1, start=False, stop=True).then_inc(d_o, 1)
                        if i == 7:
                            pe.wait_ge(d_on, q + 1)
                            for t in range(NT):
                                last = nc.tensor.transpose(PS[:, 4, t * P:(t + 1) * P], o_diff[:, t, :], ident[:])
                            last.then_inc(d_oT, 1)

            def multiply_out(n, i, hi, lo):
                pe.wait_ge(lo_ready, n + i + 1)
                for c in range(KB):
                    k = KB * (i - CB) + c
                    for t in range(NT):
                        s = slice(t * P, (t + 1) * P)
                        nc.tensor.matmul(ACC[1][:, t, :], hi[:, k, s], w_hi[i % RING][:, c, :], start=k == 0, stop=False)
                        nc.tensor.matmul(ACC[1][:, t, :], hi[:, k, s], w_lo[i % RING][:, c, :], start=False, stop=False)
                        last = nc.tensor.matmul(ACC[1][:, t, :], lo[:, k, s], w_hi[i % RING][:, c, :], start=False, stop=k == HK - 1)
                last.then_inc(block_done, 1)

            pe.wait_ge(turned_read, T_MERGE)
            pe.wait_ge(evacuated[1], E_BR)
            for r in range(3):
                branch_step(r, 0, None)
                with pe.Fori(1, NCH) as j:
                    branch_step(r, j, j - 1)

            for c in range(NCH):
                acc = ACC[c % 2]
                pe.wait_ge(evacuated[c % 2], E_O + c // 2)
                for i in range(CB):
                    if c == 0:
                        pe.wait_ge(turned_read, T_MERGE + i // 2 + 1)
                    multiply(N_O + CB * c, i, CB, mixT_hi, mixT_lo, lambda t: acc[:, t, :])
                    if i == 1 and c == 0:
                        turn_merged(T_MERGE + NCH - 1)

            def up_turn(k, parity, count):
                pe.wait_ge(evacuated[parity], count)
                pe.wait_ge(turned_read, k)
                turn(up_stage, TURN, turned_done)

            def up_step(j, jp):
                n = N_UP + 2 * CB * j
                pe.wait_ge(evacuated[0], E_UP + j)
                for i in range(CB):
                    if jp is None and i % 2 == 0:
                        pe.wait_ge(prep_lo, 2 * NCH + i // 2 + 1)
                    multiply(n, i, CB, h2_hi, h2_lo, lambda t: ACC[0][:, t, :])
                    if i == 1 and jp is not None:
                        up_turn(T_UP + 2 * jp + 1, 1, E_UP + jp + 1)
                pe.wait_ge(evacuated[1], E_UP + j)
                for i in range(CB):
                    multiply(n + CB, i, CB, h2_hi, h2_lo, lambda t: ACC[1][:, t, :])
                    if i == 1:
                        up_turn(T_UP + 2 * j, 0, E_UP + j + 1)

            for g in range(NCH):
                if g % 2:
                    pe.wait_ge(turned_read, T_UP)
                if g >= 2:
                    pe.wait_ge(prep_lo, 2 * NCH + g - 1)
                pe.wait_ge(x_new, g + 1)
                turn(x_res[:, :, g * CW:(g + 1) * CW], (SCORE_T, TURN)[g % 2], prep_turned)
            up_step(0, None)
            with pe.Fori(1, NUP) as j:
                up_step(j, j - 1)

            def down_chunk(j, acc):
                for i in range(DB):
                    if isinstance(j, int) and i % 2 == 0:
                        pe.wait_ge(act_lo_done, i // 2 + 1)
                    multiply(N_DN + DBV * j, i, DB, act_hi, act_lo, acc, 1 if i < DB - 1 else 1 + DBV - DB)
                    if i == 1 and isinstance(j, int):
                        up_turn(T_UP + 2 * NUP - 1, 1, E_UP + NUP)

            pe.wait_ge(evacuated[0], E_DN)
            down_chunk(0, lambda t: PS[:, t, :])
            pe.wait_ge(turned_read, T_UP + 2 * NUP)
            with pe.Fori(1, NCH) as j:
                down_chunk(j, lambda t: PS[:, bass.ds(NT * j + t, 1), :].rearrange("p a n -> p (a n)"))


_INS = ['x', 'mem', 'g_mix_pre', 'w_in', 'w_gate', 'b_gate', 'conv_w', 'w_conv_out', 'lambda_q1', 'lambda_k1',
        'lambda_q2', 'lambda_k2', 'g_diff_sub', 'w_diff_out', 'g_mem', 'w_mem_kv', 'w_cross_out', 'w_o',
        'g_mix_post', 'g_ffn_pre', 'w_up', 'ffn_conv_w', 'w_down', 'g_ffn_post']


def kernel(**inputs):
    import numpy as _np
    import concourse.bacc as _bacc
    from concourse import mybir as _mybir
    from concourse.bass_utils import run_bass_kernel_spmd as _run

    nc = _bacc.Bacc("TRN2", target_bir_lowering=False, num_devices=1)
    arrays, args = {}, []
    for name in _INS:
        a = _np.ascontiguousarray(inputs[name])
        arrays[f"in_{name}_dram"] = a
        args.append(nc.dram_tensor(f"in_{name}_dram", a.shape, _mybir.dt.from_np(a.dtype), kind="ExternalInput").ap())
    out = nc.dram_tensor("out_0_dram", inputs["x"].shape, _mybir.dt.float32, kind="ExternalOutput").ap()
    build_block_kernel(nc, *args, out)
    r = _run(nc, [arrays], core_ids=[0])
    return r.results[0]["out_0_dram"]
```

```python
from contextlib import ExitStack

import concourse.bass as bass
from concourse import mybir

F32 = mybir.dt.float32
F32R = mybir.dt.float32r
ALU = mybir.AluOpType
ACT = mybir.ActivationFunctionType
AX = mybir.AxisListType

P = 128
NT = 2
TOK = NT * P
CW = 512
BPC = CW // P
KB = 2
RING = 4
EPS = 1e-6
LAMBDA_INIT = 0.8 - 0.6 * 1.0
AHEAD = 1


def build_block_kernel(nc, x, mem, g_mix_pre, w_in, w_gate, b_gate, conv_w, w_conv_out,
                       lambda_q1, lambda_k1, lambda_q2, lambda_k2, g_diff_sub, w_diff_out,
                       g_mem, w_mem_kv, w_cross_out, w_o, g_mix_post,
                       g_ffn_pre, w_up, ffn_conv_w, w_down, g_ffn_post, out):
    D = x.shape[2]
    CONV = conv_w.shape[2]
    FF = w_down.shape[1]
    CROSS = w_cross_out.shape[1]
    DIFF = w_diff_out.shape[1]
    DH, DQK = 8, 64
    CH, CHD = 4, CROSS // 4
    DK = D // P
    HK = CONV // P
    FK = FF // P
    NCH = D // CW
    NUP = FF // CW
    GATE_OF = (0, 2, 1)
    assert x.shape[1] == TOK and mem.shape[1] == TOK and DIFF == DH * P and CONV == DIFF == CROSS

    in_cols = {"cb": 0, "cc": CONV, "cv": 2 * CONV, "dq": 3 * CONV, "dk": 4 * CONV, "dv": 5 * CONV, "xq": 6 * CONV}
    proj = [("mv", 0), ("mv", 1), ("mk", 0), ("mk", 1), ("xq", 0), ("xq", 1),
            ("cc", 0), ("cv", 0), ("cc", 1), ("cv", 1), ("cb", 0), ("cb", 1),
            ("dq", 0), ("dq", 1), ("dk", 0), ("dk", 1), ("dv", 0), ("dv", 1)]
    NP = len(proj)
    turned = [p for p in proj if p[0] in ("mk", "xq", "cv", "cb", "dq", "dk")]
    TI = {p: k for k, p in enumerate(turned)}
    X_PREP = [(1, 7), (2, 7), (3, 7), (4, 5)]
    CROSS_STEP = 7
    T_MERGE = len(turned)
    T_UP = T_MERGE + NCH

    CB = DK // KB
    OB = HK // KB
    DB = FK // KB
    DBV = -(-DB // RING) * RING
    SB = CB + OB
    N_BR = NP * CB
    N_O = N_BR + 3 * NCH * SB
    N_UP = N_O + NCH * CB
    N_DN = N_UP + 2 * NUP * CB
    E_BR = NP // 2
    E_O = E_BR + 3 * NCH
    E_UP = E_O + NCH // 2
    E_DN = E_UP + NUP

    with ExitStack() as ctx:
        def sem(name):
            return ctx.enter_context(nc.semaphore(name))

        K = 1024
        base = -(-nc.sbuf_base // 32) * 32
        CONST, CONST_SIZE = 48 * K, 3 * K + 512
        RA = CONST + CONST_SIZE
        RB = RA + 32 * K
        RD = RB + 32 * K
        RC = RD + 76 * K
        ctx.enter_context(nc.sbuf_tensor("arena", [P, (RC + 16 * K) // 4], F32))

        def at(name, offset, shape, dt=F32):
            return nc.alloc_sbuf_tensor_at(name, shape, dt, offset=base + offset)

        raw = [at(f"raw{s}", 4 * K * s, [P, KB, CW]) for s in range(RING)]
        w_hi = [at(f"w_hi{s}", 16 * K + 4 * K * s, [P, KB, CW], F32R) for s in range(RING)]
        w_lo = [at(f"w_lo{s}", 32 * K + 4 * K * s, [P, KB, CW], F32R) for s in range(RING)]

        cpos = [CONST]

        def const(name, shape):
            n = 4
            for d in shape[1:]:
                n *= d
            o = cpos[0]
            cpos[0] += -(-n // 32) * 32
            assert cpos[0] <= CONST + CONST_SIZE
            return at(name, o, shape)

        ident = const("ident", [P, P])
        NV = 2 * DK + 3 * HK + 1
        gmem_v = const("gmem_v", [P, DK])
        vecs = const("vecs", [P, NV])
        up_taps = const("up_taps", [P, 3, 2 * FK])
        g_sub = const("g_sub", [P, 1])
        minus_half = const("minus_half", [P, NT])
        lam_dots = const("lam_dots", [P, 2])
        lam_exp = const("lam_exp", [P, 2])
        minus_lam = const("minus_lam", [P, 1])
        sq_mem = const("sq_mem", [P, NT])
        sq_x = const("sq_x", [P, NT])
        mean_sq = const("mean_sq", [P, NT])
        r_mem = const("r_mem", [P, NT])
        r_x = const("r_x", [P, NT])
        r_mix = const("r_mix", [P, NT])
        r_h2 = const("r_h2", [P, NT])
        r_out = const("r_out", [P, NT])
        sq_part = const("sq_part", [P, NT, NCH])
        sq_mix = const("sq_mix", [P, NT])
        sq_h2 = const("sq_h2", [P, NT])
        sq_part2 = const("sq_part2", [P, NT, NCH])
        sq_down = const("sq_down", [P, NT])
        top = const("top", [P, NT, 2])
        neg_top = const("neg_top", [P, NT, 2])
        psum_e = const("psum_e", [P, NT, 2])
        inv_e = const("inv_e", [P, NT, 2])
        lam_inv = const("lam_inv", [P, NT])
        sq_o = const("sq_o", [P, NT])
        ms_o = const("ms_o", [P, NT])
        r_o = const("r_o", [P, NT])
        table_warm = const("table_warm", [P, NT])
        g_pre_v, g_ffn_v = vecs[:, 0:DK], vecs[:, DK:2 * DK]
        taps_v = vecs[:, 2 * DK:2 * DK + 3 * HK]

        hT_hi = at("hT_hi", RA, [P, DK, TOK], F32R)
        hT_lo = at("hT_lo", RA + 16 * K, [P, DK, TOK], F32R)
        h2_hi, h2_lo = hT_hi, hT_lo
        y_down = at("y_down", RA, [P, NT, D])
        g_last = at("g_last", RA + 16 * K, [P, D])
        memT_hi = at("memT_hi", RB, [P, DK, TOK], F32R)
        memT_lo = at("memT_lo", RB + 16 * K, [P, DK, TOK], F32R)
        qT = at("qT", RB, [P, HK, TOK])
        kT = at("kT", RB + 8 * K, [P, HK, TOK])
        v_tok = at("v_tok", RB + 16 * K, [P, NT, DIFF])
        xqT = at("xqT", RB + 24 * K, [P, HK, TOK])
        mixT_hi = at("mixT_hi", RB, [P, DK, TOK], F32R)
        mixT_lo = at("mixT_lo", RB + 16 * K, [P, DK, TOK], F32R)
        mem_sb = at("mem_sb", RC, [P, NT, D])
        y_conv_hi = at("y_conv_hi", RC, [P, HK, TOK], F32R)
        y_conv_lo = at("y_conv_lo", RC + 8 * K, [P, HK, TOK], F32R)
        x_res = at("x_res", RC, [P, NT, D])
        x_sb = at("x_sb", RD, [P, NT, D])
        y_diff_hi = at("y_diff_hi", RD, [P, HK, TOK], F32R)
        y_diff_lo = at("y_diff_lo", RD + 8 * K, [P, HK, TOK], F32R)
        y_mix = at("y_mix", RD, [P, NT, D])
        mkT = at("mkT", RD + 16 * K, [P, HK, TOK])
        mv_tok = at("mv_tok", RD + 24 * K, [P, NT, CROSS])
        merged = at("merged", RD + 16 * K, [P, NT, D])
        stage = at("stage", RD + 32 * K, [P, NT, CW])
        y_cross_hi = at("y_cross_hi", RD + 36 * K, [P, HK, TOK], F32R)
        y_cross_lo = at("y_cross_lo", RD + 44 * K, [P, HK, TOK], F32R)
        g_post = at("g_post", RD + 36 * K, [P, D])
        cc_sb = at("cc_sb", RD + 52 * K, [P, NT, CW])
        convT = at("convT", RD + 56 * K, [P, HK, TOK])
        y_tmp = at("y_tmp", RD + 64 * K, [P, BPC, TOK])
        p_cross = at("p_cross", RD + 68 * K, [P, NT, TOK])
        p_crossT = at("p_crossT", RD + 70 * K, [P, NT, TOK])
        gmem_rows = at("gmem_rows", RD + 70 * K, [P, P])
        vec_rows = at("vec_rows", RD + 52 * K, [P, P])
        up_rows = at("up_rows", RD + 53 * K, [P, 3, P])
        lam_rows = at("lam_rows", RD + 55 * K, [P, 4, DQK])
        lam_prod = at("lam_prod", RD + 56 * K, [P, 2, DQK])
        gate_pre = at("gate_pre", RD + 52 * K, [P, NT, CW])
        gate_tanh = at("gate_tanh", RD + 56 * K, [P, NT, CW])
        gated = at("gated", RD + 60 * K, [P, NT, CW])
        bias_bc = at("bias_bc", RD + 64 * K, [P, CW])
        qk_head = at("qk_head", RD + 66 * K, [P, 2, TOK])
        p_diff = at("p_diff", RD + 68 * K, [P, 2, 3 * P])
        a_diff = at("a_diff", RD + 71 * K, [P, 3 * P])
        a_diffT = at("a_diffT", RD + 71 * K + 1536, [P, 3 * P])
        o_diff = at("o_diff", RD + 74 * K, [P, NT, P])
        junk = at("junk", RD + 60 * K, [P, CW])
        junk_wide = at("junk_wide", RD + 60 * K, [P, D])
        act_hi = at("act_hi", RB, [P, FK, TOK], F32R)
        act_lo = at("act_lo", RB + 44 * K, [P, FK, TOK], F32R)
        up_stage = at("up_stage", RB + 88 * K, [P, NT, CW])
        conv_g = at("conv_g", RB + 92 * K, [P, BPC, TOK])
        conv_v = at("conv_v", RB + 96 * K, [P, BPC, TOK])
        prod = at("prod", RB + 100 * K, [P, BPC, TOK])
        down_junk = at("down_junk", RB + 104 * K, [P, CW])

        PS = ctx.enter_context(nc.psum_tensor("PS", [P, 8, CW], F32))
        ACC = [PS[:, 0:2, :], PS[:, 2:4, :]]
        TURN = PS[:, 4:6, :].rearrange("p b (c t) -> p (b c) t", t=TOK)
        SCORE = PS[:, 6:8, :]
        SCORE_T = PS[:, 6:8, :].rearrange("p b (c t) -> p (b c) t", t=TOK)

        mem_in = [sem(f"mem_in{g}") for g in range(NCH)]
        x_in = [sem(f"x_in{g}") for g in range(NCH)]
        gmem_in, vec_in, lam_in, up_rows_in = (sem(n) for n in ("gmem_in", "vec_in", "lam_in", "up_rows_in"))
        bias_in, xres_in, gpost_in, glast_in = (sem(n) for n in ("bias_in", "xres_in", "gpost_in", "glast_in"))
        raw_in = [sem(f"raw_in{s}") for s in range(RING)]
        stream_pace = sem("stream_pace")
        norm_pace = sem("norm_pace")
        hi_ready = sem("hi_ready")
        lo_ready = sem("lo_ready")
        block_done = sem("block_done")
        evacuated = [sem("evacuated0"), sem("evacuated1")]
        ident_ready, zero_ready, const_turned, const_ready = (sem(n) for n in ("ident_ready", "zero_ready", "const_turned", "const_ready"))
        prep_turned, prep_hi, prep_lo = (sem(n) for n in ("prep_turned", "prep_hi", "prep_lo"))
        squares = sem("squares")
        rms_ready = sem("rms_ready")
        rms_mean = sem("rms_mean")
        lam_mul, lam_dot, lam_e, lam_ready = (sem(n) for n in ("lam_mul", "lam_dot", "lam_e", "lam_ready"))
        turned_done = sem("turned_done")
        turned_read = sem("turned_read")
        tap0, tap1 = sem("tap0"), sem("tap1")
        yconv_hi, yconv_lo = sem("yconv_hi"), sem("yconv_lo")
        x_scores, x_top, x_exp, x_norm, x_inv = (sem(n) for n in ("x_scores", "x_top", "x_exp", "x_norm", "x_inv"))
        x_pT, x_pT_sb, x_oT, x_hi, x_lo, x_max = (sem(n) for n in ("x_pT", "x_pT_sb", "x_oT", "x_hi", "x_lo", "x_max"))
        d_qk, d_scores, d_mask, d_max, d_top, d_exp = (sem(n) for n in ("d_qk", "d_scores", "d_mask", "d_max", "d_top", "d_exp"))
        d_inv, d_scaled, d_a, d_aT, d_aT_sb, d_o = (sem(n) for n in ("d_inv", "d_scaled", "d_a", "d_aT", "d_aT_sb", "d_o"))
        d_sq, d_ms, d_r, d_on, d_oT, d_hi, d_lo = (sem(n) for n in ("d_sq", "d_ms", "d_r", "d_on", "d_oT", "d_hi", "d_lo"))
        gate_ready, gated_sum, mix_hi = (sem(n) for n in ("gate_ready", "gated_sum", "mix_hi"))
        mix_sq, mix_sum, x_new, h2_sq = (sem(n) for n in ("mix_sq", "mix_sum", "x_new", "h2_sq"))
        silu_done, prod_done, act_hi_done, act_lo_done = (sem(n) for n in ("silu_done", "prod_done", "act_hi_done", "act_lo_done"))
        down_sq, down_y, down_sum, out_ready, out_stored = (sem(n) for n in ("down_sq", "down_y", "down_sum", "out_ready", "out_stored"))

        block = ctx.enter_context(nc.Block())

        def cols(w, k0, c0):
            return w[0, k0 * P:(k0 + KB) * P, bass.ds(c0, CW)].rearrange("(c p) n -> p c n", p=P)

        def down_landed(j, i):
            per_chunk = len(range(i % RING, DB, RING))
            return 4 * N_DN + 16 * (j * per_chunk + i // RING + 1)

        @block.sync
        def _(sp):
            def load(n, i, w, k0, c0):
                if not isinstance(n, int) or n + i >= RING:
                    sp.wait_ge(lo_ready, n + i - RING + 1)
                    if not isinstance(n, int):
                        sp.sem_inc(stream_pace, 1)
                sp.dma_start(raw[i % RING][:], cols(w, k0, c0)).then_inc(raw_in[i % RING], 16)

            def constants():
                for dst, src in ((vec_rows[0:DK, :], g_mix_pre[0].rearrange("(b p) -> b p", p=P)),
                                 (vec_rows[DK:2 * DK, :], g_ffn_pre[0].rearrange("(b p) -> b p", p=P)),
                                 (vec_rows[2 * DK:2 * DK + 3 * HK, :], conv_w[0].rearrange("k (b p) -> (k b) p", p=P)),
                                 (vec_rows[2 * DK + 3 * HK:NV, :], g_diff_sub)):
                    sp.dma_start(dst, src).then_inc(vec_in, 16)
                sp.dma_start(up_rows[0:2 * FK, :, :], ffn_conv_w[0].rearrange("k (b p) -> b k p", p=P)).then_inc(up_rows_in, 16)
                for n, l in enumerate((lambda_q1, lambda_k1, lambda_q2, lambda_k2)):
                    sp.dma_start(lam_rows[:, n, :], l[0].partition_broadcast(P)).then_inc(lam_in, 16)

            for c, (name, half) in enumerate(proj):
                for i in range(CB):
                    if c == 0 and i < NCH:
                        sp.dma_start(mem_sb[:, :, i * CW:(i + 1) * CW],
                                     mem[0, :, i * CW:(i + 1) * CW].rearrange("(t p) n -> p t n", p=P)).then_inc(mem_in[i], 16)
                    if name == "mk":
                        load(c * CB, i, w_mem_kv, i * KB, half * CW)
                    elif name == "mv":
                        load(c * CB, i, w_mem_kv, i * KB, CROSS + half * CW)
                    else:
                        load(c * CB, i, w_in, i * KB, in_cols[name] + half * CW)
                    if c == 0 and i == NCH - 1:
                        constants()
                    if c == 0 and i >= NCH:
                        g = i - NCH
                        sp.dma_start(x_sb[:, :, g * CW:(g + 1) * CW],
                                     x[0, :, g * CW:(g + 1) * CW].rearrange("(t p) n -> p t n", p=P)).then_inc(x_in[g], 16)

            def branch_step(r, j):
                q = NCH * r + j
                n = N_BR + SB * q
                for i in range(CB):
                    load(n, i, w_gate, i * KB, GATE_OF[r] * D + j * CW)
                    if r == 1 and isinstance(j, int) and i in (5, 7):
                        t = (5, 7).index(i)
                        sp.wait_ge(block_done, N_BR + SB * NCH)
                        sp.dma_start(x_res[:, t, :], x[0, t * P:(t + 1) * P, :]).then_inc(xres_in, 16)
                    if i == 4:
                        sp.wait_ge(evacuated[0], E_BR + q)
                        if not isinstance(q, int):
                            sp.sem_inc(stream_pace, 1)
                        sp.dma_start(bias_bc[:], b_gate[0, bass.ds(GATE_OF[r] * D + j * CW, CW)].partition_broadcast(P)).then_inc(bias_in, 16)
                for i in range(OB):
                    load(n, CB + i, (w_conv_out, w_cross_out, w_diff_out)[r], i * KB, j * CW)

            for r in range(3):
                branch_step(r, 0)
                if r == 2:
                    sp.wait_ge(block_done, N_BR + SB * 2 * NCH)
                    sp.dma_start(g_post[:], g_mix_post[0, :].partition_broadcast(P)).then_inc(gpost_in, 16)
                with sp.Fori(1, NCH) as j:
                    branch_step(r, j)
            for j in range(NCH):
                for i in range(CB):
                    load(N_O + j * CB, i, w_o, i * KB, j * CW)
            with sp.Fori(0, NUP) as j:
                for i in range(CB):
                    load(N_UP + 2 * CB * j, i, w_up, i * KB, j * CW)
                for i in range(CB):
                    load(N_UP + 2 * CB * j, CB + i, w_up, i * KB, FF + j * CW)

            def down_chunk(j):
                for i in range(DB):
                    load(N_DN + DBV * j, i, w_down, i * KB, j * CW)
                    if i == 6 and isinstance(j, int):
                        sp.wait_ge(block_done, N_DN)
                        sp.dma_start(g_last[:], g_ffn_post[0, :].partition_broadcast(P)).then_inc(glast_in, 16)

            down_chunk(0)
            with sp.Fori(1, NCH) as j:
                down_chunk(j)
            for g in range(NCH):
                for t in range(NT):
                    sp.wait_ge(out_ready, NT * g + t + 1)
                    sp.dma_start(out[0, t * P:(t + 1) * P, g * CW:(g + 1) * CW],
                                 y_down[:, t, g * CW:(g + 1) * CW]).then_inc(out_stored, 16)
            sp.wait_ge(out_stored, 16 * NT * NCH)

        @block.gpsimd
        def _(pool):
            nc.gpsimd.memset(ident[:], 0.0).then_inc(zero_ready, 1)
            nc.gpsimd.memset(minus_half[:], -0.5).then_inc(zero_ready, 1)
            pool.wait_ge(zero_ready, 2)
            nc.gpsimd.affine_select(out=ident[:], in_=ident[:], compare_op=ALU.not_equal, fill=1.0, base=0,
                                    pattern=[[-1, P]], channel_multiplier=1).then_inc(ident_ready, 1)
            rms_count = [0]

            def rms(dst, sums, width):
                nc.gpsimd.tensor_scalar(mean_sq[:], sums, 1.0 / width, EPS, ALU.mult, ALU.add).then_inc(rms_mean, 1)
                rms_count[0] += 1
                pool.wait_ge(rms_mean, rms_count[0])
                nc.gpsimd.tensor_tensor(dst, mean_sq[:], minus_half[:], ALU.pow).then_inc(rms_ready, 1)
                pool.wait_ge(rms_ready, rms_count[0])

            pool.wait_ge(squares, 2)
            rms(r_mem[:], sq_mem[:], D)
            pool.wait_ge(squares, 4)
            rms(r_x[:], sq_x[:], D)

            def head(h):
                if not (isinstance(h, int) and h == 0):
                    pool.wait_ge(d_scores, h)
                nc.gpsimd.tensor_copy(qk_head[:, 0, :], qT[:, bass.ds(h, 1), :])
                nc.gpsimd.tensor_copy(qk_head[:, 1, :], kT[:, bass.ds(h, 1), :]).then_inc(d_qk, 1)
                pool.wait_ge(d_sq, h + 1)
                pool.sem_inc(norm_pace, 1)
                nc.gpsimd.tensor_scalar(ms_o[:], sq_o[:], 1.0 / P, EPS, ALU.mult, ALU.add).then_inc(d_ms, 1)
                pool.wait_ge(d_ms, h + 1)
                nc.gpsimd.tensor_tensor(r_o[:], ms_o[:], minus_half[:], ALU.pow).then_inc(d_r, 1)
                pool.wait_ge(d_r, h + 1)

            pool.wait_ge(turned_read, T_MERGE)
            pool.wait_ge(x_lo, CH)
            head(0)
            with pool.Fori(1, DH) as h:
                head(h)

            pool.wait_ge(mix_sum, 1)
            rms(r_mix[:], sq_mix[:], D)
            pool.wait_ge(h2_sq, 1)
            rms(r_h2[:], sq_h2[:], D)
            pool.wait_ge(down_sum, 1)
            rms(r_out[:], sq_down[:], D)

        @block.scalar
        def _(act):
            act.dma_start(gmem_rows[0:DK, :], g_mem[0].rearrange("(b p) -> b p", p=P)).then_inc(gmem_in, 16)
            act.sem_inc(down_sq, AHEAD)
            act.wait_ge(zero_ready, 2)
            nc.scalar.activation(table_warm[:], minus_half[:], ACT.Exp)

            def split(n, i, landed=None, inc=1):
                act.wait_ge(raw_in[i % RING], 4 * n + 16 * (i // RING + 1) if landed is None else landed)
                if not isinstance(n, int) or n + i >= RING:
                    act.wait_ge(block_done, n + i - RING + 1)
                nc.scalar.activation(w_hi[i % RING][:], raw[i % RING][:], ACT.Copy).then_inc(hi_ready, inc)

            def prepare(G, g, src, gains, dst):
                act.wait_ge(prep_turned, G + 1)
                for b in range(BPC):
                    last = nc.scalar.activation(dst[:, BPC * g + b, :], src[:, b, :], ACT.Copy,
                                                scale=gains[:, BPC * g + b:BPC * g + b + 1])
                    if b % KB == KB - 1:
                        last.then_inc(prep_hi, 1)

            def row_squares(n, src, dst, t):
                if n:
                    act.wait_ge(squares, n)
                nc.scalar.activation(junk_wide[:], src[:, t, :], ACT.Square, accum_out=dst[:, t:t + 1]).then_inc(squares, 1)

            def evacuate(c, n_end, dst, scale):
                act.wait_ge(block_done, n_end)
                for t in range(NT):
                    last = nc.scalar.activation(dst[:, t, :], ACC[c % 2][:, t, :], ACT.Copy, scale=scale[:, t:t + 1])
                last.then_inc(evacuated[c % 2], 1)

            def after_projection(c):
                name, half = proj[c]
                s = slice(half * CW, (half + 1) * CW)
                n_end = (c + 1) * CB
                if c == 0:
                    act.wait_ge(rms_ready, 1)
                if c == 4:
                    act.wait_ge(rms_ready, 2)
                if name == "mv":
                    evacuate(c, n_end, mv_tok[:, :, s], r_mem)
                elif name == "dv":
                    evacuate(c, n_end, v_tok[:, :, s], r_x)
                elif name == "cc":
                    if half:
                        act.wait_ge(evacuated[(c - 1) % 2], (c - 1) // 2 + 1)
                    evacuate(c, n_end, cc_sb, r_x)
                elif name != "cv":
                    if TI[proj[c]]:
                        act.wait_ge(turned_done, TI[proj[c]])
                    evacuate(c, n_end, stage, r_mem if name == "mk" else r_x)

            def first_tap(k, dst, taps):
                act.wait_ge(turned_done, k + 1)
                for b in range(BPC):
                    last = nc.scalar.activation(dst[:, b, :], TURN[:, b, :], ACT.Copy, scale=taps[b])
                last.then_inc(tap0, 1)

            def cross_exp(h):
                act.wait_ge(x_top, h + 1)
                for t in range(NT):
                    last = nc.scalar.activation(p_cross[:, t, :], PS[:, 6, t * TOK:(t + 1) * TOK], ACT.Exp,
                                                bias=neg_top[:, 0, t:t + 1], scale=CHD ** -0.5,
                                                accum_out=psum_e[:, 0, t:t + 1])
                last.then_inc(x_exp, 1)

            act.wait_ge(const_ready, 1)
            prepare(0, 0, TURN, gmem_v, memT_hi)
            for c, (name, half) in enumerate(proj):
                for i in range(CB):
                    split(c * CB, i)
                    if i == 3 and c:
                        after_projection(c - 1)
                    if c == 0 and i in (1, 3, 5):
                        g = (i + 1) // 2
                        prepare(g, g, (TURN, SCORE_T)[g % 2], gmem_v, memT_hi)
                    if c == 0 and i >= 6:
                        row_squares(i - 6, mem_sb, sq_mem, i - 6)
                    if (c, i) in X_PREP:
                        g = X_PREP.index((c, i))
                        if g == 0:
                            act.wait_ge(const_ready, 3)
                        prepare(NCH + g, g, SCORE_T, g_pre_v, hT_hi)
                    if c == 1 and i in (4, 5):
                        if i == 4:
                            for g in range(NCH):
                                act.wait_ge(x_in[g], 16)
                        row_squares(i - 2, x_sb, sq_x, i - 4)
                    if c == 1 and i == 6:
                        act.wait_ge(lam_dot, 1)
                        nc.scalar.activation(lam_exp[:], lam_dots[:], ACT.Exp).then_inc(lam_e, 1)
                    if i == 5 and c and proj[c - 1][0] == "cv":
                        hp = proj[c - 1][1]
                        first_tap(TI[proj[c - 1]], convT[:, BPC * hp:BPC * (hp + 1), :],
                                  [taps_v[:, 2 * HK + BPC * hp + b:2 * HK + BPC * hp + b + 1] for b in range(BPC)])
                    if i == 6 and c and proj[c - 1][0] == "cb":
                        hp = proj[c - 1][1]
                        act.wait_ge(turned_read, TI[proj[c - 1]] + 1)
                        nc.scalar.activation(y_conv_hi[:, BPC * hp:BPC * (hp + 1), :], y_tmp[:], ACT.Copy).then_inc(yconv_hi, 1)
                    h = c - CROSS_STEP
                    if 0 <= h < CH:
                        if i == 4:
                            cross_exp(h)
                        if i == 7:
                            act.wait_ge(x_pT, h + 1)
                            nc.scalar.activation(p_crossT[:], PS[:, 7, :].rearrange("p (a b) -> p a b", a=NT), ACT.Copy).then_inc(x_pT_sb, 1)
                            act.wait_ge(x_oT, h + 1)
                            nc.scalar.activation(y_cross_hi[:, 2 * h:2 * h + 2, :],
                                                 PS[:, 6, :].rearrange("p (a b) -> p a b", a=2), ACT.Copy).then_inc(x_hi, 1)

            def merge_hi(j):
                act.wait_ge(turned_done, T_MERGE + j + 1)
                nc.scalar.activation(mixT_hi[:, bass.ds(BPC * j, BPC), :], TURN, ACT.Copy, scale=0.5).then_inc(mix_hi, 1)

            def branch_step(r, j, jp):
                q = NCH * r + j
                n = N_BR + SB * q
                for i in range(SB):
                    split(n, i)
                    if i == 3 and isinstance(q, int) and q == 0:
                        after_projection(NP - 1)
                    if i == 5 and r == 2 and jp is not None:
                        merge_hi(jp)
                    if r < 2:
                        if i == 4:
                            act.wait_ge(d_top, q + 1)
                            for t, (s0, s1) in enumerate(((0, P), (P, 3 * P))):
                                for m in range(2):
                                    last = nc.scalar.activation(p_diff[:, m, s0:s1], SCORE[:, m, s0:s1], ACT.Exp,
                                                                bias=neg_top[:, t, m:m + 1], scale=DQK ** -0.5,
                                                                accum_out=psum_e[:, t, m:m + 1])
                            last.then_inc(d_exp, 1)
                        if i == 7:
                            act.wait_ge(d_aT, q + 1)
                            nc.scalar.activation(a_diffT[:], PS[:, 4, 0:3 * P], ACT.Copy).then_inc(d_aT_sb, 1)
                        if i == 8:
                            act.wait_ge(d_o, q + 1)
                            for t in range(NT):
                                last = nc.scalar.activation(o_diff[:, t, :], PS[:, 5, t * P:(t + 1) * P], ACT.Square,
                                                            accum_out=sq_o[:, t:t + 1])
                            last.then_inc(d_sq, 1)
                        if i == 11:
                            act.wait_ge(d_oT, q + 1)
                            nc.scalar.activation(y_diff_hi[:, bass.ds(q, 1), :], PS[:, 4, 0:TOK].rearrange("p (a t) -> p a t", a=1), ACT.Copy,
                                                 scale=g_sub[:, 0:1]).then_inc(d_hi, 1)
                    if i == 11:
                        act.wait_ge(evacuated[0], E_BR + q + 1)
                        act.wait_ge(evacuated[1], E_BR + q)
                        nc.scalar.activation(gate_tanh[:], gate_pre[:], ACT.Tanh, scale=0.5).then_inc(gate_ready, 1)

            for r in range(3):
                branch_step(r, 0, None)
                with act.Fori(1, NCH) as j:
                    branch_step(r, j, j - 1)

            def mix_squares(c):
                act.wait_ge(block_done, N_O + CB * (c + 1))
                for t in range(NT):
                    if c or t:
                        act.wait_ge(mix_sq, NT * c + t)
                    nc.scalar.activation(junk[:], ACC[c % 2][:, t, :], ACT.Square,
                                         accum_out=sq_part[:, t, c:c + 1]).then_inc(mix_sq, 1)

            for c in range(NCH):
                for i in range(CB):
                    split(N_O + CB * c, i)
                    if i == 3 and c:
                        mix_squares(c - 1)
                    if i == 5 and c == 0:
                        merge_hi(NCH - 1)

            def up_evacuate(k, n_end, parity):
                act.wait_ge(turned_done, k)
                act.wait_ge(block_done, n_end)
                for t in range(NT):
                    last = nc.scalar.activation(up_stage[:, t, :], ACC[parity][:, t, :], ACT.Copy, scale=r_h2[:, t:t + 1])
                last.then_inc(evacuated[parity], 1)

            def up_first_tap(k, dst, blk):
                act.wait_ge(turned_done, k + 1)
                for b in range(BPC):
                    last = nc.scalar.activation(dst[:, b, :], TURN[:, b, :], ACT.Copy, scale=up_taps[:, 2, bass.ds(blk + b, 1)])
                last.then_inc(tap0, 1)

            def value_done(j, i):
                if i == 3:
                    up_evacuate(T_UP + 2 * j + 1, N_UP + 2 * CB * j + 2 * CB, 1)
                if i == 5:
                    act.wait_ge(prod_done, AHEAD + j)
                    up_first_tap(T_UP + 2 * j + 1, conv_v, FK + BPC * j)
                if i == 7:
                    act.wait_ge(prod_done, AHEAD + j + 1)
                    nc.scalar.activation(act_hi[:, bass.ds(BPC * j, BPC), :], prod[:], ACT.Copy).then_inc(act_hi_done, 1)

            def up_step(j, jp):
                n = N_UP + 2 * CB * j
                for i in range(CB):
                    split(n, i)
                    if jp is not None:
                        value_done(jp, i)
                    elif i == 2:
                        mix_squares(NCH - 1)
                        for g in range(NCH):
                            prepare(2 * NCH + g, g, (SCORE_T, TURN)[g % 2], g_ffn_v, h2_hi)
                        for t in range(NT):
                            act.wait_ge(mix_sq, NT * NCH + t)
                            last = nc.scalar.activation(junk_wide[:], x_res[:, t, :], ACT.Square, accum_out=sq_h2[:, t:t + 1])
                            last.then_inc(mix_sq, 1)
                        act.wait_ge(mix_sq, NT * NCH + NT)
                for i in range(CB):
                    split(n, CB + i)
                    if i == 3:
                        if jp is None:
                            act.wait_ge(rms_ready, 4)
                        up_evacuate(T_UP + 2 * j, n + CB, 0)
                    if i == 5:
                        if jp is not None:
                            act.wait_ge(prod_done, AHEAD + j)
                        up_first_tap(T_UP + 2 * j, conv_g, BPC * j)
                    if i == 6:
                        act.wait_ge(turned_read, T_UP + 2 * j + 1)
                        nc.scalar.activation(conv_g[:], conv_g[:], ACT.Silu).then_inc(silu_done, 1)

            up_step(0, None)
            with act.Fori(1, NUP) as j:
                up_step(j, j - 1)

            def down_squares(jp):
                act.wait_ge(block_done, N_DN + DBV * (jp + 1))
                for t in range(NT):
                    act.wait_ge(down_sq, AHEAD + NT * jp + t)
                    nc.scalar.activation(down_junk[:], PS[:, bass.ds(NT * jp + t, 1), :].rearrange("p a n -> p (a n)"), ACT.Square,
                                         accum_out=sq_part2[:, t, bass.ds(jp, 1)]).then_inc(down_sq, 1)

            def down_chunk(j, jp):
                for i in range(DB):
                    split(N_DN + DBV * j, i, down_landed(j, i), 1 if i < DB - 1 else 1 + DBV - DB)
                    if jp is None:
                        value_done(NUP - 1, i)
                    elif i == 3:
                        down_squares(jp)

            down_chunk(0, None)
            with act.Fori(1, NCH) as j:
                down_chunk(j, j - 1)
            down_squares(NCH - 1)

        @block.vector
        def _(dve):
            def split(n, i, inc=1):
                dve.wait_ge(hi_ready, n + i + 1)
                nc.vector.tensor_tensor(w_lo[i % RING][:], raw[i % RING][:], w_hi[i % RING][:].bitcast(F32),
                                        ALU.subtract).then_inc(lo_ready, inc)

            def prepare(G, g, src, gains, hi, lo):
                for b in range(BPC):
                    kb = BPC * g + b
                    if b % KB == 0:
                        dve.wait_ge(prep_hi, 2 * G + b // KB + 1)
                    last = nc.vector.scalar_tensor_tensor(out=lo[:, kb, :], in0=src[:, b, :], scalar=gains[:, kb:kb + 1],
                                                          in1=hi[:, kb, :].bitcast(F32), op0=ALU.mult, op1=ALU.subtract)
                    if b % KB == KB - 1:
                        last.then_inc(prep_lo, 1)

            dve.sem_inc(prod_done, AHEAD)
            dve.sem_inc(act_lo_done, AHEAD)
            dve.wait_ge(const_turned, 1)
            nc.vector.tensor_copy(gmem_v[:], PS[:, 0, 0:DK]).then_inc(const_ready, 1)
            dve.wait_ge(const_ready, 1)
            prepare(0, 0, TURN, gmem_v, memT_hi, memT_lo)

            def constants():
                dve.wait_ge(const_turned, 2)
                nc.vector.tensor_copy(vecs[:], PS[:, 2, 0:NV]).then_inc(const_ready, 1)
                nc.vector.tensor_copy(up_taps[:], PS[:, 3, 0:6 * FK].rearrange("p (k b) -> p k b", k=3)).then_inc(const_ready, 1)
                dve.wait_ge(const_ready, 3)
                nc.vector.tensor_scalar(g_sub[:], vecs[:, NV - 1:NV], 1.0 - LAMBDA_INIT, None, ALU.mult).then_inc(const_ready, 1)
                dve.wait_ge(lam_in, 64)
                nc.vector.tensor_tensor(lam_prod[:], lam_rows[:, 0:4:2, :], lam_rows[:, 1:4:2, :], ALU.mult).then_inc(lam_mul, 1)
                dve.wait_ge(lam_mul, 1)
                nc.vector.tensor_reduce(lam_dots[:], lam_prod[:], AX.X, ALU.add).then_inc(lam_dot, 1)

            def turned_conv(k, dst, taps):
                dve.wait_ge(tap0, conv_count(k) + 1)
                for b in range(BPC):
                    last = nc.vector.scalar_tensor_tensor(out=dst[:, b, 1:TOK], in0=TURN[:, b, 0:TOK - 1], scalar=taps(1, b),
                                                          in1=dst[:, b, 1:TOK], op0=ALU.mult, op1=ALU.add)
                last.then_inc(tap1, 1)
                dve.wait_ge(tap1, conv_count(k) + 1)
                for b in range(BPC):
                    last = nc.vector.scalar_tensor_tensor(out=dst[:, b, 2:TOK], in0=TURN[:, b, 0:TOK - 2], scalar=taps(0, b),
                                                          in1=dst[:, b, 2:TOK], op0=ALU.mult, op1=ALU.add)
                last.then_inc(turned_read, 1)

            def conv_count(k):
                if isinstance(k, int) and k < T_UP:
                    return [TI[("cv", 0)], TI[("cv", 1)]].index(k)
                return k - T_UP + 2

            def after_projection(c, i):
                name, half = proj[c]
                k = TI.get(proj[c])
                s = slice(half * BPC, (half + 1) * BPC)
                if i == 3 and name == "cv":
                    dve.wait_ge(turned_done, k)
                    dve.wait_ge(evacuated[(c - 1) % 2], (c - 1) // 2 + 1)
                    dve.wait_ge(block_done, (c + 1) * CB)
                    for t in range(NT):
                        last = nc.vector.scalar_tensor_tensor(out=stage[:, t, :], in0=ACC[c % 2][:, t, :], scalar=r_x[:, t:t + 1],
                                                              in1=cc_sb[:, t, :], op0=ALU.mult, op1=ALU.mult)
                    last.then_inc(evacuated[c % 2], 1)
                if i == 5 and name == "cv":
                    turned_conv(k, convT[:, s, :], lambda m, b: taps_v[:, m * HK + half * BPC + b:m * HK + half * BPC + b + 1])
                if i == 5 and name in ("mk", "xq", "dq", "dk"):
                    dve.wait_ge(turned_done, k + 1)
                    dst = {"mk": mkT, "xq": xqT, "dq": qT, "dk": kT}[name]
                    nc.vector.tensor_copy(dst[:, s, :], TURN).then_inc(turned_read, 1)
                if i == 5 and name == "cb":
                    dve.wait_ge(turned_done, k + 1)
                    if half == 0:
                        dve.wait_ge(turned_read, TI[("cv", 1)] + 1)
                    else:
                        dve.wait_ge(yconv_lo, 1)
                    nc.vector.tensor_tensor(y_tmp[:], TURN, convT[:, s, :], ALU.mult).then_inc(turned_read, 1)
                if i == 6 and name == "cb":
                    dve.wait_ge(yconv_hi, half + 1)
                    nc.vector.tensor_tensor(y_conv_lo[:, s, :], y_tmp[:], y_conv_hi[:, s, :].bitcast(F32),
                                            ALU.subtract).then_inc(yconv_lo, 1)

            for c, (name, half) in enumerate(proj):
                for i in range(CB):
                    split(c * CB, i)
                    if c:
                        after_projection(c - 1, i)
                    if c == 0 and i in (1, 3, 5):
                        g = (i + 1) // 2
                        prepare(g, g, (TURN, SCORE_T)[g % 2], gmem_v, memT_hi, memT_lo)
                    if c == 1 and i == 0:
                        constants()
                    if (c, i) in X_PREP:
                        g = X_PREP.index((c, i))
                        prepare(NCH + g, g, SCORE_T, g_pre_v, hT_hi, hT_lo)
                    if c == 2 and i == 0:
                        dve.wait_ge(lam_e, 1)
                        nc.vector.scalar_tensor_tensor(out=minus_lam[:], in0=lam_exp[:, 1:2], scalar=LAMBDA_INIT, in1=lam_exp[:, 0:1],
                                                       op0=ALU.subtract, op1=ALU.subtract).then_inc(lam_ready, 1)
                    h = c - CROSS_STEP
                    if 0 <= h < CH:
                        if i == 3:
                            dve.wait_ge(x_scores, h + 1)
                            if h:
                                dve.wait_ge(x_exp, h)
                            nc.vector.tensor_reduce(top[:, 0, :], PS[:, 6, :].rearrange("p (t k) -> p t k", t=NT), AX.X,
                                                    ALU.max).then_inc(x_max, 1)
                            dve.wait_ge(x_max, h + 1)
                            nc.vector.tensor_scalar(neg_top[:, 0, :], top[:, 0, :], -CHD ** -0.5, None, ALU.mult).then_inc(x_top, 1)
                        if i == 5:
                            dve.wait_ge(x_exp, h + 1)
                            nc.vector.reciprocal(inv_e[:, 0, :], psum_e[:, 0, :]).then_inc(x_inv, 1)
                            dve.wait_ge(x_inv, h + 1)
                            for t in range(NT):
                                last = nc.vector.tensor_scalar(p_cross[:, t, :], p_cross[:, t, :], inv_e[:, 0, t:t + 1], None, ALU.mult)
                            last.then_inc(x_norm, 1)
                        if i == 7:
                            dve.wait_ge(x_hi, h + 1)
                            nc.vector.tensor_tensor(y_cross_lo[:, 2 * h:2 * h + 2, :], PS[:, 6, :].rearrange("p (a b) -> p a b", a=2),
                                                    y_cross_hi[:, 2 * h:2 * h + 2, :].bitcast(F32), ALU.subtract).then_inc(x_lo, 1)

            def gate_product(r, jp, q_prev):
                dve.wait_ge(block_done, N_BR + SB * (q_prev + 1))
                dve.wait_ge(gate_ready, q_prev + 1)
                first = r == 0
                for t in range(NT):
                    dst = merged[:, t, bass.ds(jp * CW, CW)] if first else gated[:, t, :]
                    last = nc.vector.scalar_tensor_tensor(out=dst, in0=gate_tanh[:, t, :], scalar=1.0, in1=ACC[1][:, t, :],
                                                          op0=ALU.add, op1=ALU.mult)
                last.then_inc(evacuated[1], 1)
                if not first:
                    dve.wait_ge(evacuated[1], E_BR + q_prev + 1)
                    m = merged[:, :, bass.ds(jp * CW, CW)]
                    if r == 2:
                        dve.wait_ge(turned_done, T_MERGE + jp)
                    nc.vector.tensor_tensor(m if r == 1 else stage[:], m, gated[:], ALU.add).then_inc(gated_sum, 1)
                    dve.wait_ge(gated_sum, q_prev - NCH + 1)

            def merge_lo(j):
                dve.wait_ge(mix_hi, j + 1)
                nc.vector.scalar_tensor_tensor(out=mixT_lo[:, bass.ds(BPC * j, BPC), :].rearrange("p a t -> p (a t)"),
                                               in0=TURN.rearrange("p a t -> p (a t)"), scalar=0.5,
                                               in1=mixT_hi[:, bass.ds(BPC * j, BPC), :].bitcast(F32).rearrange("p a t -> p (a t)"),
                                               op0=ALU.mult, op1=ALU.subtract).then_inc(turned_read, 1)

            def branch_step(r, j, rp, jp):
                q = NCH * r + j
                n = N_BR + SB * q
                for i in range(SB):
                    split(n, i)
                    if i == 3 and rp is not None:
                        gate_product(rp, jp, q - 1)
                    if i == 5 and rp == 2:
                        merge_lo(jp)
                    if r < 2:
                        if i == 3:
                            dve.wait_ge(d_scores, q + 1)
                            nc.vector.memset(SCORE[0:64, :, 64:128], -1e37)
                            nc.vector.memset(SCORE[0:64, :, 320:384], -1e37).then_inc(d_mask, 1)
                            dve.wait_ge(d_mask, q + 1)
                            nc.vector.tensor_reduce(top[:, 0, :], SCORE[:, :, 0:P], AX.X, ALU.max)
                            nc.vector.tensor_reduce(top[:, 1, :], SCORE[:, :, P:3 * P], AX.X, ALU.max).then_inc(d_max, 1)
                            dve.wait_ge(d_max, q + 1)
                            nc.vector.tensor_scalar(neg_top[:], top[:], -DQK ** -0.5, None, ALU.mult).then_inc(d_top, 1)
                        if i == 5:
                            dve.wait_ge(d_exp, q + 1)
                            nc.vector.reciprocal(inv_e[:], psum_e[:]).then_inc(d_inv, 1)
                            dve.wait_ge(d_inv, 2 * q + 1)
                            nc.vector.tensor_scalar(lam_inv[:], inv_e[:, :, 1], minus_lam[:, 0:1], None, ALU.mult).then_inc(d_inv, 1)
                            dve.wait_ge(d_inv, 2 * q + 2)
                            for t, (s0, s1) in enumerate(((0, P), (P, 3 * P))):
                                last = nc.vector.tensor_scalar(p_diff[:, 1, s0:s1], p_diff[:, 1, s0:s1], lam_inv[:, t:t + 1], None, ALU.mult)
                            last.then_inc(d_scaled, 1)
                            dve.wait_ge(d_scaled, q + 1)
                            for t, (s0, s1) in enumerate(((0, P), (P, 3 * P))):
                                last = nc.vector.scalar_tensor_tensor(out=a_diff[:, s0:s1], in0=p_diff[:, 0, s0:s1], scalar=inv_e[:, t, 0:1],
                                                                      in1=p_diff[:, 1, s0:s1], op0=ALU.mult, op1=ALU.add)
                            last.then_inc(d_a, 1)
                        if i == 9:
                            dve.wait_ge(d_r, q + 1)
                            for t in range(NT):
                                last = nc.vector.tensor_scalar(o_diff[:, t, :], PS[:, 5, t * P:(t + 1) * P], r_o[:, t:t + 1], None, ALU.mult)
                            last.then_inc(d_on, 1)
                    if i == 11:
                        dve.wait_ge(block_done, n + CB)
                        dve.wait_ge(bias_in, 16 * (q + 1))
                        if rp is not None:
                            dve.wait_ge(gate_ready, q)
                        for t in range(NT):
                            last = nc.vector.scalar_tensor_tensor(out=gate_pre[:, t, :], in0=ACC[0][:, t, :], scalar=r_x[:, t:t + 1],
                                                                  in1=bias_bc[:], op0=ALU.mult, op1=ALU.add)
                        last.then_inc(evacuated[0], 1)
                    if r < 2 and i == 11:
                        dve.wait_ge(d_hi, q + 1)
                        nc.vector.scalar_tensor_tensor(out=y_diff_lo[:, bass.ds(q, 1), :].rearrange("p a t -> p (a t)"), in0=PS[:, 4, 0:TOK],
                                                       scalar=g_sub[:, 0:1],
                                                       in1=y_diff_hi[:, bass.ds(q, 1), :].bitcast(F32).rearrange("p a t -> p (a t)"),
                                                       op0=ALU.mult, op1=ALU.subtract).then_inc(d_lo, 1)

            dve.wait_ge(lam_ready, 1)
            dve.wait_ge(const_ready, 4)
            for r in range(3):
                branch_step(r, 0, r - 1 if r else None, NCH - 1)
                with dve.Fori(1, NCH) as j:
                    branch_step(r, j, r, j - 1)

            def mix_out(c):
                if c == 0:
                    dve.wait_ge(gpost_in, 16)
                dve.wait_ge(mix_sq, NT * (c + 1))
                for t in range(NT):
                    s = slice(c * CW, (c + 1) * CW)
                    last = nc.vector.tensor_tensor(y_mix[:, t, s], ACC[c % 2][:, t, :], g_post[:, s], ALU.mult)
                last.then_inc(evacuated[c % 2], 1)

            for c in range(NCH):
                for i in range(CB):
                    split(N_O + CB * c, i)
                    if i == 3:
                        if c:
                            mix_out(c - 1)
                        else:
                            gate_product(2, NCH - 1, 3 * NCH - 1)
                    if i == 5 and c == 0:
                        merge_lo(NCH - 1)

            def value_done(j, i):
                if i == 5:
                    turned_conv(T_UP + 2 * j + 1, conv_v, lambda m, b: up_taps[:, m, bass.ds(FK + BPC * j + b, 1)])
                if i == 6:
                    dve.wait_ge(turned_read, T_UP + 2 * j + 2)
                    dve.wait_ge(silu_done, j + 1)
                    dve.wait_ge(act_lo_done, AHEAD + j)
                    nc.vector.tensor_tensor(prod[:], conv_g[:], conv_v[:], ALU.mult).then_inc(prod_done, 1)
                if i == 7:
                    dve.wait_ge(act_hi_done, j + 1)
                    nc.vector.tensor_tensor(act_lo[:, bass.ds(BPC * j, BPC), :], prod[:],
                                            act_hi[:, bass.ds(BPC * j, BPC), :].bitcast(F32), ALU.subtract).then_inc(act_lo_done, 1)

            def new_x():
                dve.wait_ge(mix_sq, NT * NCH)
                nc.vector.tensor_reduce(sq_mix[:], sq_part[:], AX.X, ALU.add).then_inc(mix_sum, 1)
                mix_out(NCH - 1)
                dve.wait_ge(evacuated[1], E_UP)
                dve.wait_ge(evacuated[0], E_UP)
                dve.wait_ge(xres_in, 16 * NT)
                dve.wait_ge(rms_ready, 3)
                for g in range(NCH + 1):
                    if g < NCH:
                        s = slice(g * CW, (g + 1) * CW)
                        for t in range(NT):
                            last = nc.vector.scalar_tensor_tensor(out=x_res[:, t, s], in0=y_mix[:, t, s], scalar=r_mix[:, t:t + 1],
                                                                  in1=x_res[:, t, s], op0=ALU.mult, op1=ALU.add)
                        last.then_inc(x_new, 1)
                    if g:
                        prepare(2 * NCH + g - 1, g - 1, (SCORE_T, TURN)[(g - 1) % 2], g_ffn_v, h2_hi, h2_lo)
                dve.wait_ge(mix_sq, NT * NCH + NT)
                nc.vector.tensor_copy(sq_mix[:], sq_h2[:]).then_inc(h2_sq, 1)

            def up_step(j, jp):
                n = N_UP + 2 * CB * j
                for i in range(CB):
                    split(n, i)
                    if jp is not None:
                        value_done(jp, i)
                    elif i == 2:
                        new_x()
                for i in range(CB):
                    split(n, CB + i)
                    if i == 5:
                        turned_conv(T_UP + 2 * j, conv_g, lambda m, b: up_taps[:, m, bass.ds(BPC * j + b, 1)])

            up_step(0, None)
            with dve.Fori(1, NUP) as j:
                up_step(j, j - 1)

            def down_out(jp):
                dve.wait_ge(down_sq, AHEAD + NT * (jp + 1))
                for t in range(NT):
                    last = nc.vector.tensor_tensor(y_down[:, t, bass.ds(jp * CW, CW)],
                                                   PS[:, bass.ds(NT * jp + t, 1), :].rearrange("p a n -> p (a n)"),
                                                   g_last[:, bass.ds(jp * CW, CW)], ALU.mult)
                last.then_inc(down_y, 1)

            def down_chunk(j, jp):
                for i in range(DB):
                    split(N_DN + DBV * j, i, 1 if i < DB - 1 else 1 + DBV - DB)
                    if jp is None:
                        value_done(NUP - 1, i)
                    elif i == 3:
                        down_out(jp)

            down_chunk(0, None)
            dve.wait_ge(glast_in, 16)
            with dve.Fori(1, NCH) as j:
                down_chunk(j, j - 1)
            dve.wait_ge(down_sq, AHEAD + NT * NCH)
            nc.vector.tensor_reduce(sq_down[:], sq_part2[:], AX.X, ALU.add).then_inc(down_sum, 1)
            down_out(NCH - 1)
            dve.wait_ge(down_y, NCH)
            dve.wait_ge(rms_ready, 5)
            for g in range(NCH):
                s = slice(g * CW, (g + 1) * CW)
                for t in range(NT):
                    nc.vector.scalar_tensor_tensor(out=y_down[:, t, s], in0=y_down[:, t, s], scalar=r_out[:, t:t + 1],
                                                   in1=x_res[:, t, s], op0=ALU.mult, op1=ALU.add).then_inc(out_ready, 1)

        @block.tensor
        def _(pe):
            def multiply(n, i, nblk, hi, lo, acc, inc=1):
                pe.wait_ge(lo_ready, n + i + 1)
                for c in range(KB):
                    k = KB * i + c
                    first, last_k = k == 0, k == KB * nblk - 1
                    for t in range(NT):
                        s = slice(t * P, (t + 1) * P)
                        o = acc(t)
                        a_hi, a_lo, b_hi, b_lo = hi[:, k, s], lo[:, k, s], w_hi[i % RING][:, c, :], w_lo[i % RING][:, c, :]
                        nc.tensor.matmul(o, a_hi, b_hi, start=first, stop=False)
                        nc.tensor.matmul(o, a_hi, b_lo, start=False, stop=False)
                        last = nc.tensor.matmul(o, a_lo, b_hi, start=False, stop=last_k)
                last.then_inc(block_done, inc)

            def turn(src, dst, signal):
                for t in range(NT):
                    for b in range(BPC):
                        last = nc.tensor.transpose(dst[:, b, t * P:(t + 1) * P], src[:, t, b * P:(b + 1) * P], ident[:])
                last.then_inc(signal, 1)

            pe.wait_ge(ident_ready, 1)
            pe.wait_ge(gmem_in, 16)
            nc.tensor.transpose(PS[:, 0, 0:DK], gmem_rows[0:DK, :], ident[0:DK, 0:DK]).then_inc(const_turned, 1)

            def turn_memory(g):
                if g >= 2:
                    pe.wait_ge(prep_lo, 2 * (g - 1))
                pe.wait_ge(mem_in[g], 16)
                turn(mem_sb[:, :, g * CW:(g + 1) * CW], (TURN, SCORE_T)[g % 2], prep_turned)

            def turn_constants():
                pe.wait_ge(vec_in, 64)
                pe.wait_ge(up_rows_in, 16)
                nc.tensor.transpose(PS[:, 2, 0:NV], vec_rows[0:NV, :], ident[0:NV, 0:NV])
                for k in range(3):
                    last = nc.tensor.transpose(PS[:, 3, k * 2 * FK:(k + 1) * 2 * FK], up_rows[0:2 * FK, k, :], ident[0:2 * FK, 0:2 * FK])
                last.then_inc(const_turned, 1)

            turn_memory(0)
            turn_memory(1)
            pe.wait_ge(const_ready, 1)

            for c, (name, half) in enumerate(proj):
                acc = ACC[c % 2]
                if c >= 2:
                    pe.wait_ge(evacuated[c % 2], c // 2)
                elif c == 1:
                    pe.wait_ge(const_ready, 3)
                on_mem = name in ("mk", "mv")
                for i in range(CB):
                    if c == 0 or c == NCH:
                        pe.wait_ge(prep_lo, (0 if c == 0 else 2 * NCH) + i + 1)
                    multiply(c * CB, i, CB, memT_hi if on_mem else hT_hi, memT_lo if on_mem else hT_lo, lambda t: acc[:, t, :])
                    if i == 1 and c and proj[c - 1] in TI:
                        k = TI[proj[c - 1]]
                        pe.wait_ge(evacuated[(c - 1) % 2], (c - 1) // 2 + 1)
                        if k:
                            pe.wait_ge(turned_read, k)
                        turn(stage, TURN, turned_done)
                    if c == 0 and i in (0, 2):
                        turn_memory(2 + i // 2)
                    if c == 0 and i == CB - 1:
                        turn_constants()
                    if (c, i + 4) in X_PREP:
                        g = X_PREP.index((c, i + 4))
                        pe.wait_ge(x_in[g], 16)
                        pe.wait_ge(prep_lo, 2 * (NCH + g))
                        turn(x_sb[:, :, g * CW:(g + 1) * CW], SCORE_T, prep_turned)
                    h = c - CROSS_STEP
                    if 0 <= h < CH:
                        if i == 0:
                            if h:
                                pe.wait_ge(x_lo, h)
                            pe.wait_ge(turned_read, TI[("xq", 1)] + 1)
                            for t in range(NT):
                                for kk in range(2):
                                    last = nc.tensor.matmul(PS[:, 6, t * TOK:(t + 1) * TOK], xqT[:, 2 * h + kk, t * P:(t + 1) * P],
                                                            mkT[:, 2 * h + kk, :], start=kk == 0, stop=kk == 1)
                            last.then_inc(x_scores, 1)
                        if i == 3:
                            pe.wait_ge(x_norm, h + 1)
                            for kb in range(NT):
                                for t in range(NT):
                                    last = nc.tensor.transpose(PS[:, 7, kb * TOK + t * P:kb * TOK + (t + 1) * P],
                                                               p_cross[:, t, kb * P:(kb + 1) * P], ident[:])
                            last.then_inc(x_pT, 1)
                        if i == 4:
                            pe.wait_ge(x_pT_sb, h + 1)
                            for db in range(2):
                                for kb in range(NT):
                                    v0 = h * CHD + db * P
                                    last = nc.tensor.matmul(PS[:, 6, db * TOK:(db + 1) * TOK], mv_tok[:, kb, v0:v0 + P],
                                                            p_crossT[:, kb, :], start=kb == 0, stop=kb == NT - 1)
                            last.then_inc(x_oT, 1)

            def turn_merged(k):
                pe.wait_ge(gated_sum, k - T_MERGE + NCH + 1)
                pe.wait_ge(turned_read, k)
                turn(stage, TURN, turned_done)

            def branch_step(r, j, jp):
                q = NCH * r + j
                n = N_BR + SB * q
                pe.wait_ge(evacuated[0], E_BR + q)
                for i in range(SB):
                    if i < CB:
                        multiply(n, i, CB, hT_hi, hT_lo, lambda t: ACC[0][:, t, :])
                    else:
                        if i == CB:
                            pe.wait_ge(evacuated[1], E_BR + q)
                            pe.wait_ge(*((yconv_lo, 2), (x_lo, CH), (d_lo, DH))[r])
                        y_hi, y_lo = ((y_conv_hi, y_conv_lo), (y_cross_hi, y_cross_lo), (y_diff_hi, y_diff_lo))[r]
                        multiply_out(n, i, y_hi, y_lo)
                    if i == 1 and r == 2 and jp is not None:
                        turn_merged(T_MERGE + jp)
                    if r < 2:
                        if i == 0:
                            pe.wait_ge(d_qk, q + 1)
                            for m in range(2):
                                s = slice(m * DQK, (m + 1) * DQK)
                                nc.tensor.matmul(PS[:, 6 + m, 0:P], qk_head[s, 0, 0:P], qk_head[s, 1, 0:P], start=True, stop=True)
                                last = nc.tensor.matmul(PS[:, 6 + m, P:3 * P], qk_head[s, 0, P:2 * P], qk_head[s, 1, :], start=True, stop=True)
                            last.then_inc(d_scores, 1)
                        if i == 3:
                            pe.wait_ge(d_a, q + 1)
                            for b in range(3):
                                last = nc.tensor.transpose(PS[:, 4, b * P:(b + 1) * P], a_diff[:, b * P:(b + 1) * P], ident[:])
                            last.then_inc(d_aT, 1)
                        if i == 4:
                            pe.wait_ge(d_aT_sb, q + 1)
                            if isinstance(q, int) and q == 0:
                                pe.wait_ge(evacuated[1], E_BR)
                            v0, v1 = (v_tok[:, kb, bass.ds(q * P, P)] for kb in range(2))
                            nc.tensor.matmul(PS[:, 5, 0:P], a_diffT[:, 0:P], v0, start=True, stop=True)
                            nc.tensor.matmul(PS[:, 5, P:2 * P], a_diffT[:, P:2 * P], v0, start=True, stop=False)
                            nc.tensor.matmul(PS[:, 5, P:2 * P], a_diffT[:, 2 * P:3 * P], v1, start=False, stop=True).then_inc(d_o, 1)
                        if i == 7:
                            pe.wait_ge(d_on, q + 1)
                            for t in range(NT):
                                last = nc.tensor.transpose(PS[:, 4, t * P:(t + 1) * P], o_diff[:, t, :], ident[:])
                            last.then_inc(d_oT, 1)

            def multiply_out(n, i, hi, lo):
                pe.wait_ge(lo_ready, n + i + 1)
                for c in range(KB):
                    k = KB * (i - CB) + c
                    for t in range(NT):
                        s = slice(t * P, (t + 1) * P)
                        nc.tensor.matmul(ACC[1][:, t, :], hi[:, k, s], w_hi[i % RING][:, c, :], start=k == 0, stop=False)
                        nc.tensor.matmul(ACC[1][:, t, :], hi[:, k, s], w_lo[i % RING][:, c, :], start=False, stop=False)
                        last = nc.tensor.matmul(ACC[1][:, t, :], lo[:, k, s], w_hi[i % RING][:, c, :], start=False, stop=k == HK - 1)
                last.then_inc(block_done, 1)

            pe.wait_ge(turned_read, T_MERGE)
            for r in range(3):
                branch_step(r, 0, None)
                with pe.Fori(1, NCH) as j:
                    branch_step(r, j, j - 1)

            for c in range(NCH):
                acc = ACC[c % 2]
                pe.wait_ge(evacuated[c % 2], E_O + c // 2)
                for i in range(CB):
                    if c == 0:
                        pe.wait_ge(turned_read, T_MERGE + i // 2 + 1)
                    multiply(N_O + CB * c, i, CB, mixT_hi, mixT_lo, lambda t: acc[:, t, :])
                    if i == 1 and c == 0:
                        turn_merged(T_MERGE + NCH - 1)

            def up_turn(k, parity, count):
                pe.wait_ge(evacuated[parity], count)
                pe.wait_ge(turned_read, k)
                turn(up_stage, TURN, turned_done)

            def up_step(j, jp):
                n = N_UP + 2 * CB * j
                pe.wait_ge(evacuated[0], E_UP + j)
                for i in range(CB):
                    if jp is None:
                        pe.wait_ge(prep_lo, 4 * NCH + i + 1)
                    multiply(n, i, CB, h2_hi, h2_lo, lambda t: ACC[0][:, t, :])
                    if i == 1 and jp is not None:
                        up_turn(T_UP + 2 * jp + 1, 1, E_UP + jp + 1)
                pe.wait_ge(evacuated[1], E_UP + j)
                for i in range(CB):
                    multiply(n + CB, i, CB, h2_hi, h2_lo, lambda t: ACC[1][:, t, :])
                    if i == 1:
                        up_turn(T_UP + 2 * j, 0, E_UP + j + 1)

            for g in range(NCH):
                if g % 2:
                    pe.wait_ge(turned_read, T_UP)
                if g >= 2:
                    pe.wait_ge(prep_lo, 4 * NCH + 2 * (g - 1))
                pe.wait_ge(x_new, g + 1)
                turn(x_res[:, :, g * CW:(g + 1) * CW], (SCORE_T, TURN)[g % 2], prep_turned)
            up_step(0, None)
            with pe.Fori(1, NUP) as j:
                up_step(j, j - 1)

            def down_chunk(j, acc):
                for i in range(DB):
                    if isinstance(j, int) and i % 2 == 0:
                        pe.wait_ge(act_lo_done, AHEAD + i // 2 + 1)
                    multiply(N_DN + DBV * j, i, DB, act_hi, act_lo, acc, 1 if i < DB - 1 else 1 + DBV - DB)
                    if i == 1 and isinstance(j, int):
                        up_turn(T_UP + 2 * NUP - 1, 1, E_UP + NUP)

            pe.wait_ge(evacuated[0], E_DN)
            down_chunk(0, lambda t: PS[:, t, :])
            pe.wait_ge(turned_read, T_UP + 2 * NUP)
            with pe.Fori(1, NCH) as j:
                down_chunk(j, lambda t: PS[:, bass.ds(NT * j + t, 1), :].rearrange("p a n -> p (a n)"))


_INS = ['x', 'mem', 'g_mix_pre', 'w_in', 'w_gate', 'b_gate', 'conv_w', 'w_conv_out', 'lambda_q1', 'lambda_k1',
        'lambda_q2', 'lambda_k2', 'g_diff_sub', 'w_diff_out', 'g_mem', 'w_mem_kv', 'w_cross_out', 'w_o',
        'g_mix_post', 'g_ffn_pre', 'w_up', 'ffn_conv_w', 'w_down', 'g_ffn_post']


def kernel(**inputs):
    import numpy as _np
    import concourse.bacc as _bacc
    from concourse import mybir as _mybir
    from concourse.bass_utils import run_bass_kernel_spmd as _run

    nc = _bacc.Bacc("TRN2", target_bir_lowering=False, num_devices=1)
    arrays, args = {}, []
    for name in _INS:
        a = _np.ascontiguousarray(inputs[name])
        arrays[f"in_{name}_dram"] = a
        args.append(nc.dram_tensor(f"in_{name}_dram", a.shape, _mybir.dt.from_np(a.dtype), kind="ExternalInput").ap())
    out = nc.dram_tensor("out_0_dram", inputs["x"].shape, _mybir.dt.float32, kind="ExternalOutput").ap()
    build_block_kernel(nc, *args, out)
    r = _run(nc, [arrays], core_ids=[0])
    return r.results[0]["out_0_dram"]
```
